# Optimizing a Trainium2 kernel written in Bass

```python
import math
import jax, jax.numpy as jnp
from jax import lax
import numpy as np

D_MODEL = 1024
BATCH = 1
SEQ = 256
DEPTH = 2

HEAD_DIM = 64
ROPE_THETA = 10000.0
NORM_EPS = 1e-6
Q_BLOCK = 128

MLA_HEADS = 6
MLA_Q_RANK = 384
MLA_KV_RANK = 256
MLA_NOPE_DIM = 64
MLA_ROPE_DIM = 32
MLA_V_DIM = 64

SWA_HEADS = 6
SWA_KV_HEADS = 2
WINDOW = 128

DIFF_HEADS = 4
DIFF_QK_DIM = 32
DIFF_V_DIM = 64

MIX_WIDTH = MLA_HEADS * MLA_V_DIM + SWA_HEADS * HEAD_DIM + DIFF_HEADS * DIFF_V_DIM

IN_SPLITS = (
    MLA_Q_RANK, MLA_KV_RANK, MLA_ROPE_DIM,
    SWA_HEADS * HEAD_DIM, SWA_KV_HEADS * HEAD_DIM, SWA_KV_HEADS * HEAD_DIM,
    DIFF_HEADS * 2 * DIFF_QK_DIM, DIFF_HEADS * 2 * DIFF_QK_DIM, DIFF_HEADS * DIFF_V_DIM,
)
IN_WIDTH = sum(IN_SPLITS)

N_GROUPS = 4
EXPERTS_PER_GROUP = 8
TOP_K = 2
EXPERT_FF = 256

kernel_name = "hymba_style_mla_swa_diff_hmoe_encoder"

def rms_norm(x, g):
    xf = x.astype(jnp.float32)
    y = xf * lax.rsqrt(jnp.mean(xf * xf, axis=-1, keepdims=True) + NORM_EPS)
    return (y * g.astype(jnp.float32)).astype(x.dtype)

def rope_tables(seq, dim):
    inv = 1.0 / (ROPE_THETA ** (jnp.arange(0, dim, 2, dtype=jnp.float32) / dim))
    ang = jnp.arange(seq, dtype=jnp.float32)[:, None] * inv[None, :]
    return jnp.cos(ang), jnp.sin(ang)

def apply_rope(x, cos, sin):
    shape = (cos.shape[0],) + (1,) * (x.ndim - 3) + (cos.shape[1],)
    c = cos.reshape(shape).astype(x.dtype)
    s = sin.reshape(shape).astype(x.dtype)
    x1, x2 = jnp.split(x, 2, axis=-1)
    return jnp.concatenate([x1 * c - x2 * s, x2 * c + x1 * s], axis=-1)

def sweep_query_blocks(fn, *qs):
    B, S = qs[0].shape[:2]
    nb = S // Q_BLOCK
    blocked = tuple(jnp.moveaxis(q.reshape((B, nb, Q_BLOCK) + q.shape[2:]), 1, 0) for q in qs)
    out = lax.map(lambda args: fn(*args), blocked)
    return jnp.moveaxis(out, 0, 1).reshape((B, S) + out.shape[3:])

def mla_mixer(c_q, c_kv, k_rope, q_norm, kv_norm, w_uq, w_ukv, rope):
    B, S, _ = c_q.shape
    q = (rms_norm(c_q, q_norm) @ w_uq).reshape(B, S, MLA_HEADS, MLA_NOPE_DIM + MLA_ROPE_DIM)
    q_nope = q[..., :MLA_NOPE_DIM]
    q_rope = apply_rope(q[..., MLA_NOPE_DIM:], *rope)
    kv = (rms_norm(c_kv, kv_norm) @ w_ukv).reshape(B, S, MLA_HEADS, MLA_NOPE_DIM + MLA_V_DIM)
    k_nope = kv[..., :MLA_NOPE_DIM]
    v = kv[..., MLA_NOPE_DIM:]
    k_rope = apply_rope(k_rope, *rope)
    scale = (MLA_NOPE_DIM + MLA_ROPE_DIM) ** -0.5

    def block(qn, qr):
        s = (jnp.einsum('bqhd,bkhd->bhqk', qn, k_nope)
             + jnp.einsum('bqhr,bkr->bhqk', qr, k_rope))
        p = jax.nn.softmax(s.astype(jnp.float32) * scale, axis=-1)
        return jnp.einsum('bhqk,bkhd->bqhd', p.astype(v.dtype), v)

    o = sweep_query_blocks(block, q_nope, q_rope)
    return o.reshape(B, S, MLA_HEADS * MLA_V_DIM)

def swa_mixer(q, k, v, sink, rope):
    B, S, _ = q.shape
    G = SWA_HEADS // SWA_KV_HEADS
    nb = S // WINDOW
    q = apply_rope(q.reshape(B, S, SWA_HEADS, HEAD_DIM), *rope)
    k = apply_rope(k.reshape(B, S, SWA_KV_HEADS, HEAD_DIM), *rope)
    v = v.reshape(B, S, SWA_KV_HEADS, HEAD_DIM)
    qb = q.reshape(B, nb, WINDOW, SWA_KV_HEADS, G, HEAD_DIM)

    def band(t):
        tp = jnp.pad(t, ((0, 0), (WINDOW, WINDOW), (0, 0), (0, 0)))
        tp = tp.reshape(B, nb + 2, WINDOW, SWA_KV_HEADS, HEAD_DIM)
        return jnp.concatenate([tp[:, :-2], tp[:, 1:-1], tp[:, 2:]], axis=2)

    kb, vb = band(k), band(v)
    s = jnp.einsum('bnqhgd,bnkhd->bnhgqk', qb, kb).astype(jnp.float32) * (HEAD_DIM ** -0.5)
    a = jnp.arange(WINDOW)[:, None]
    c = jnp.arange(3 * WINDOW)[None, :]
    rel = c - a
    in_window = (rel >= 0) & (rel <= 2 * WINDOW)
    key_pos = jnp.arange(nb)[:, None] * WINDOW - WINDOW + jnp.arange(3 * WINDOW)[None, :]
    in_range = (key_pos >= 0) & (key_pos < S)
    valid = in_window[None] & in_range[:, None, :]
    s = jnp.where(valid[None, :, None, None], s, -jnp.inf)
    sink_logit = jnp.broadcast_to(
        sink.astype(jnp.float32).reshape(1, 1, SWA_KV_HEADS, G, 1, 1), s.shape[:-1] + (1,))
    p = jax.nn.softmax(jnp.concatenate([s, sink_logit], axis=-1), axis=-1)[..., :-1]
    o = jnp.einsum('bnhgqk,bnkhd->bnqhgd', p.astype(vb.dtype), vb)
    return o.reshape(B, S, SWA_HEADS * HEAD_DIM)

def diff_mixer(q, k, v, lq1, lk1, lq2, lk2, subln, lambda_init, rope):
    B, S, _ = q.shape
    q = apply_rope(q.reshape(B, S, DIFF_HEADS, 2, DIFF_QK_DIM), *rope)
    k = apply_rope(k.reshape(B, S, DIFF_HEADS, 2, DIFF_QK_DIM), *rope)
    v = v.reshape(B, S, DIFF_HEADS, DIFF_V_DIM)
    lam = (jnp.exp(jnp.sum(lq1.astype(jnp.float32) * lk1.astype(jnp.float32)))
           - jnp.exp(jnp.sum(lq2.astype(jnp.float32) * lk2.astype(jnp.float32)))
           + lambda_init)
    scale = DIFF_QK_DIM ** -0.5

    def block(qb):
        s = jnp.einsum('bqhcd,bkhcd->bhcqk', qb, k)
        p = jax.nn.softmax(s.astype(jnp.float32) * scale, axis=-1)
        attn = p[:, :, 0] - lam * p[:, :, 1]
        return jnp.einsum('bhqk,bkhd->bqhd', attn.astype(v.dtype), v)

    o = sweep_query_blocks(block, q)
    o = rms_norm(o, subln) * (1.0 - lambda_init)
    return o.reshape(B, S, DIFF_HEADS * DIFF_V_DIM)

def hier_moe(h, w_rg, b_rg, w_re, b_re, w_gate, w_up, w_down):
    B, S, D = h.shape
    t = h.reshape(B * S, D)
    T = t.shape[0]
    g_logits = (t @ w_rg).astype(jnp.float32) + b_rg.astype(jnp.float32)
    g_prob = jax.nn.softmax(g_logits, axis=-1)
    g_idx = jnp.argmax(g_logits, axis=-1)
    g_gate = jnp.take_along_axis(g_prob, g_idx[:, None], axis=-1)
    e_logits = ((t @ w_re).astype(jnp.float32) + b_re.astype(jnp.float32)).reshape(
        T, N_GROUPS, EXPERTS_PER_GROUP)
    e_in = jnp.take_along_axis(e_logits, g_idx[:, None, None], axis=1)[:, 0]
    top_val, top_idx = lax.top_k(e_in, TOP_K)
    top_w = jax.nn.softmax(top_val, axis=-1) * g_gate
    comb_e = jnp.sum(jax.nn.one_hot(top_idx, EXPERTS_PER_GROUP) * top_w[..., None], axis=1)
    comb = (jax.nn.one_hot(g_idx, N_GROUPS)[:, :, None] * comb_e[:, None, :]).astype(t.dtype)
    y = jnp.zeros_like(t)
    for g in range(N_GROUPS):
        a = jnp.einsum('td,edf->tef', t, w_gate[g])
        u = jnp.einsum('td,edf->tef', t, w_up[g])
        hid = jax.nn.silu(a) * u * comb[:, g, :, None]
        y = y + jnp.einsum('tef,efd->td', hid, w_down[g])
    return y.reshape(B, S, D)

def _split_points():
    pts, acc = [], 0
    for w in IN_SPLITS[:-1]:
        acc += w
        pts.append(acc)
    return pts

def setup_inputs(seed: int = 0) -> dict:
    key = jax.random.key(seed)
    ks = jax.random.split(key, 32)

    def nrm(k, shape, scale):
        return jax.random.normal(k, shape, jnp.float32) * scale

    def gain(k, shape):
        return 1.0 + 0.02 * jax.random.normal(k, shape, jnp.float32)

    L, D, E, G, F = DEPTH, D_MODEL, EXPERTS_PER_GROUP, N_GROUPS, EXPERT_FF
    return {
        "x": nrm(ks[0], (BATCH, SEQ, D), 1.0),
        "attn_norm": gain(ks[1], (L, D)),
        "w_in": nrm(ks[2], (L, D, IN_WIDTH), D ** -0.5),
        "mla_q_norm": gain(ks[3], (L, MLA_Q_RANK)),
        "mla_kv_norm": gain(ks[4], (L, MLA_KV_RANK)),
        "mla_w_uq": nrm(ks[5], (L, MLA_Q_RANK, MLA_HEADS * (MLA_NOPE_DIM + MLA_ROPE_DIM)), MLA_Q_RANK ** -0.5),
        "mla_w_ukv": nrm(ks[6], (L, MLA_KV_RANK, MLA_HEADS * (MLA_NOPE_DIM + MLA_V_DIM)), MLA_KV_RANK ** -0.5),
        "swa_sink": nrm(ks[7], (L, SWA_HEADS), 0.5),
        "diff_lq1": nrm(ks[8], (L, DIFF_QK_DIM), 0.1),
        "diff_lk1": nrm(ks[9], (L, DIFF_QK_DIM), 0.1),
        "diff_lq2": nrm(ks[10], (L, DIFF_QK_DIM), 0.1),
        "diff_lk2": nrm(ks[11], (L, DIFF_QK_DIM), 0.1),
        "diff_subln": gain(ks[12], (L, DIFF_V_DIM)),
        "w_out": nrm(ks[13], (L, MIX_WIDTH, D), MIX_WIDTH ** -0.5),
        "ffn_norm": gain(ks[14], (L, D)),
        "router_group": nrm(ks[15], (L, D, G), D ** -0.5),
        "router_group_bias": nrm(ks[16], (L, G), 0.01),
        "router_expert": nrm(ks[17], (L, D, G * E), D ** -0.5),
        "router_expert_bias": nrm(ks[18], (L, G * E), 0.01),
        "w_gate": nrm(ks[19], (L, G, E, D, F), D ** -0.5),
        "w_up": nrm(ks[20], (L, G, E, D, F), D ** -0.5),
        "w_down": nrm(ks[21], (L, G, E, F, D), F ** -0.5),
        "final_norm": gain(ks[22], (D,)),
    }

def reference(x, attn_norm, w_in, mla_q_norm, mla_kv_norm, mla_w_uq, mla_w_ukv, swa_sink,
              diff_lq1, diff_lk1, diff_lq2, diff_lk2, diff_subln, w_out, ffn_norm,
              router_group, router_group_bias, router_expert, router_expert_bias,
              w_gate, w_up, w_down, final_norm):
    S = x.shape[1]
    rope32 = rope_tables(S, MLA_ROPE_DIM)
    rope64 = rope_tables(S, HEAD_DIM)
    points = _split_points()
    for l in range(DEPTH):
        h = rms_norm(x, attn_norm[l])
        (mq, mkv, mkr, sq, sk, sv, dq, dk, dv) = jnp.split(h @ w_in[l], points, axis=-1)
        o_mla = mla_mixer(mq, mkv, mkr, mla_q_norm[l], mla_kv_norm[l], mla_w_uq[l], mla_w_ukv[l], rope32)
        o_swa = swa_mixer(sq, sk, sv, swa_sink[l], rope64)
        lambda_init = 0.8 - 0.6 * math.exp(-0.3 * l)
        o_diff = diff_mixer(dq, dk, dv, diff_lq1[l], diff_lk1[l], diff_lq2[l], diff_lk2[l],
                            diff_subln[l], lambda_init, rope32)
        x = x + jnp.concatenate([o_mla, o_swa, o_diff], axis=-1) @ w_out[l]
        x = x + hier_moe(rms_norm(x, ffn_norm[l]), router_group[l], router_group_bias[l],
                         router_expert[l], router_expert_bias[l], w_gate[l], w_up[l], w_down[l])
    return rms_norm(x, final_norm)


_drawn_inputs = setup_inputs


def setup_inputs(seed=0):
    import zlib

    import numpy as np

    out = dict(_drawn_inputs(seed))
    spreads = {}
    factors = {'mla_q_norm': 7.172,
     'mla_kv_norm': 5.093,
     'swa_sink': 63.103,
     'router_group_bias': 10.818,
     'final_norm': 22.618,
     'diff_subln': 3.912,
     'router_expert_bias': 3.796}
    for name, (base, spread) in spreads.items():
        noise = np.random.default_rng([zlib.crc32(name.encode()), seed]).standard_normal(out[name].shape)
        drawn = base * np.exp(spread * noise) if base else spread * noise
        out[name] = __import__('jax').numpy.asarray(drawn.astype(out[name].dtype))
    for name, factor in factors.items():
        out[name] = (out[name] * factor).astype(out[name].dtype)
    return out
```

```python
import math

import concourse.bass as bass
import concourse.mybir as mybir
import numpy as np
from concourse.alu_op_type import AluOpType as ALU

F32 = mybir.dt.float32
I32 = mybir.dt.int32
U32 = mybir.dt.uint32
ACT = mybir.ActivationFunctionType
AX = mybir.AxisListType.X

P = 128
D = 1024
T = 256
TT = T // P
L = 2
KD = D // P
EPS = 1e-6

MLA_H, MLA_QR, MLA_KVR, NOPE, ROPE, MLA_V = 6, 384, 256, 64, 32, 64
MLA_QK = NOPE + ROPE
SWA_H, SWA_KV, HD, WINDOW = 6, 2, 64, 128
DIFF_H, DQK, DV = 4, 32, 64
IN_W = MLA_QR + MLA_KVR + ROPE + SWA_H * HD + 2 * SWA_KV * HD + 4 * DIFF_H * DQK + DIFF_H * DV
NMAPS = MLA_H + SWA_H + 2 * DIFF_H

G, E, F = 4, 8, 256
NE = G * E
NPAIR = NE // 2
SLOTS = 64
NIT = NPAIR // 2
NEG = -3.0e38

C_Q, C_KV, C_SQK, C_VDQ, C_DKV = (0, 384), (384, 288), (672, 512), (1184, 384), (1568, 512)
assert C_DKV[0] + C_DKV[1] == IN_W

O_ID, O_TRI, O_ONE, O_IOTA = 0, P, 2 * P, 3 * P
O_C64 = O_IOTA + SLOTS
O_C32 = O_C64 + 3 * TT * 32
O_MASK = O_C32 + 3 * TT * 16
O_LAM = O_MASK + TT * T
N_CONST = O_LAM + 2 * L


def constants():
    c = np.zeros((P, N_CONST), np.float32)
    c[:, O_ID:O_ID + P] = np.eye(P)
    c[:, O_TRI:O_TRI + P] = np.triu(np.ones((P, P)), 1)
    c[:, O_ONE:O_ONE + P] = 1.0
    c[:, O_IOTA:O_IOTA + SLOTS] = np.arange(SLOTS)
    for off, dim in ((O_C64, 64), (O_C32, 32)):
        inv = (np.float32(1.0) / (np.float32(10000.0) ** (np.arange(0, dim, 2, dtype=np.float32) / np.float32(dim))))
        ang = np.arange(T, dtype=np.float32)[:, None] * inv[None, :].astype(np.float32)
        h = dim // 2
        for n, t in enumerate((np.cos(ang), np.sin(ang), -np.sin(ang))):
            for tt in range(TT):
                c[:, off + (n * TT + tt) * h:off + (n * TT + tt + 1) * h] = t[tt * P:(tt + 1) * P]
    q = np.arange(T).reshape(TT, P).T[:, :, None]
    c[:, O_MASK:O_MASK + TT * T] = np.where(np.abs(q - np.arange(T)[None, None]) <= WINDOW, 0.0, -1e30).reshape(P, TT * T)
    for l in range(L):
        init = 0.8 - 0.6 * math.exp(-0.3 * l)
        c[:, O_LAM + l] = init
        c[:, O_LAM + L + l] = 1.0 - init
    return c


def encoder_kernel(nc, const, x_in, attn_norm, w_in, mla_q_norm, mla_kv_norm, w_uq, w_ukv, swa_sink, lq1, lk1, lq2, lk2,
                   diff_subln, w_out, ffn_norm, router_group, router_group_bias, router_expert, router_expert_bias,
                   w_gate, w_up, w_down, final_norm, out):
    def sb(name, shape, dt=F32):
        return nc.alloc_sbuf_tensor(name, shape, dt)

    ps = nc.alloc_psum_tensor("banks", [P, 8, 512], F32)

    ring = sb("ring", [P, 14, IN_W])
    cst = sb("cst", [P, N_CONST])
    g_attn = sb("g_attn", [P, L, KD])
    g_ffn = sb("g_ffn", [P, L, KD])
    g_low = sb("g_low", [P, L, 5])
    sink = sb("sink", [P, L, SWA_H])
    nsink = sb("nsink", [P, L, SWA_H])
    lqk = sb("lqk", [P, 4, L, DQK])
    subln = sb("subln", [P, L])
    sublg = sb("sublg", [P, L])
    rbias = sb("rbias", [P, L, G + NE])
    w_r = sb("w_r", [P, L, KD, G + NE])
    w_rl = sb("w_rl", [P, KD, G + NE])
    g_fin = sb("g_fin", [P, D])

    x = sb("x", [P, TT, D])
    hA = sb("hA", [P, TT, KD, P])
    hAf = hA[:, :, :, :].rearrange("p t k j -> p (t k j)")
    hT = sb("hT", [P, KD, T])
    shared = sb("shared", [P, 4992])
    qTm = shared[:, 0:1536].rearrange("p (h t) -> p h t", h=MLA_H)
    kTm = shared[:, 1536:3072].rearrange("p (h t) -> p h t", h=MLA_H)
    lowT = shared[:, 1536:2816].rearrange("p (c t) -> p c t", c=5)
    km = shared[:, 3072:4224].rearrange("p (t h d) -> p t h d", t=TT, h=MLA_H)
    vm = shared[:, 4224:4992].rearrange("p (t d) -> p t d", t=TT)
    hTg = shared[:, 0:1024].rearrange("p (k s) -> p k s", k=KD)
    pick = shared[:, 1024:1280].rearrange("p (t s) -> p t s", t=TT)
    pickT = shared[:, 1280:1536]
    sil = [shared[:, 1536:1792], shared[:, 1792:2048]]
    hid = [shared[:, 2048:2304], shared[:, 2304:2560]]
    hidT = [shared[:, 2560 + 256 * n:2816 + 256 * n].rearrange("p (j s) -> p j s", j=2) for n in range(2)]
    y_sb = shared[:, 3072:4096].rearrange("p (b n) -> p b n", b=2)
    low = sb("low", [P, TT, MLA_QR + MLA_KVR])
    qm = low[:, :, 0:MLA_H * MLA_QK].rearrange("p t (h d) -> p t h d", h=MLA_H)
    rq = sb("rq", [P, TT, D])
    vsd = sb("vsd", [P, TT, SWA_KV * HD + DIFF_H * DV])
    kro = sb("kro", [P, TT, ROPE])
    qTs = sb("qTs", [P, 3, T])
    kps = sb("kps", [P, SWA_KV, T])
    qTd = sb("qTd", [P, 2, T])
    kpd = sb("kpd", [P, 2 * DIFF_H, T])
    ms = sb("ms", [P, TT, T])
    msf = ms[:, :, :].rearrange("p t n -> p (t n)")
    logitT = msf[0:G + NE, 0:T]
    tmpA = [hAf[:, 0:512], hAf[:, 1024:1536]]
    tmpB = [hAf[:, 512:1024], hAf[:, 1536:2048]]
    prob = [hAf[:, 512 * n:512 * n + 512].rearrange("p (t k) -> p t k", t=TT) for n in range(4)]
    rqf = rq[:, :, :].rearrange("p t n -> p (t n)")
    probT = [rqf[:, 512 * n:512 * n + 512].rearrange("p (k t) -> p k t", k=TT) for n in range(4)]
    odiff = low[:, :, 0:DIFF_H * DV]
    nhalf = sb("nhalf", [P, 8])
    ssq = sb("ssq", [P, TT])
    rs = sb("rs", [P, TT])
    ssc = sb("ssc", [P, 4])
    rsc = sb("rsc", [P, 4])
    dssq = sb("dssq", [P, 8])
    drs = sb("drs", [P, 8])
    lam = sb("lam", [P, 4])
    neglam = sb("neglam", [P, 1])
    nmax = sb("nmax", [P, NMAPS, TT])
    rmax = sb("rmax", [P, NMAPS, TT])
    psum_ = sb("psum_", [P, NMAPS, TT])
    esink = sb("esink", [P, SWA_H, TT])
    rinv = sb("rinv", [P, NMAPS, TT])
    gl8 = sb("gl8", [P, TT, 8])
    el = sb("el", [P, TT, NE])
    prod = sb("prod", [P, TT, G, E])
    gtop = sb("gtop", [P, TT, 8])
    gidx = sb("gidx", [P, TT, 8], U32)
    etop = sb("etop", [P, TT, 8])
    eidx = sb("eidx", [P, TT, 8], U32)
    fidx = sb("fidx", [P, 2, TT, 8])
    esel = sb("esel", [P, TT, E])
    ngm = sb("ngm", [P, TT])
    gsum = sb("gsum", [P, TT])
    gexp = sb("gexp", [P, TT, G])
    wts = sb("wts", [P, 5, TT])
    ohg = sb("ohg", [P, TT, G])
    oh = sb("oh", [P, 5, TT, E])
    pmax = sb("pmax", [P, TT, 4])
    member = sb("member", [P, TT, NPAIR])
    key = sb("key", [P, TT, NPAIR + 2])
    comb = sb("comb", [P, TT, NE + 4])
    cc = sb("cc", [P, 2])
    cnt = sb("cnt", [P, 4])
    npass_t = sb("npass_t", [P, 1], I32)

    ident = cst[:, O_ID:O_ID + P]
    tri = cst[:, O_TRI:O_TRI + P]
    ones = cst[:, O_ONE:O_ONE + P]
    iota = cst[:, O_IOTA:O_IOTA + SLOTS]
    mask = cst[:, O_MASK:O_MASK + TT * T].rearrange("p (t k) -> p t k", t=TT)

    def table(dim, which, tt):
        off, h = (O_C64, 32) if dim == 64 else (O_C32, 16)
        return cst[:, off + (which * TT + tt) * h:off + (which * TT + tt + 1) * h]

    s = {n: nc.alloc_semaphore(n) for n in (
        "params_landed", "router_landed", "const_landed", "x_landed", "cleared", "sublg_ready",
        "landed_a", "landed_b", "landed_da", "landed_db", "landed_uq", "landed_ukv", "landed_wo",
        "freed_a", "freed_b", "freed_da", "freed_db", "freed_up",
        "sq_act", "sq_dve", "rms_ready", "h_act", "h_dve", "passed", "hT_ps", "hT_sb",
        "u_ps", "low_sq", "low_rms", "low_ready", "v_sb", "rope_mul", "rope_add", "lowT_ps", "lowT_sb",
        "up_ps", "q_nope", "kv_sb", "krope_sb", "T_ps", "T_act", "T_dve", "lam_sum", "lam_exp",
        "score_ps", "nmax_ready", "prob_ready", "probT_ps", "probT_act", "probT_dve", "o_ps", "o_sb",
        "dsq_ready", "drms_ready", "dnorm_ready", "oT_ps", "oT_dve", "scaled", "wout_ps", "x_mixed",
        "logit_ps", "logitT_ps", "logitT_sb", "rt_dve", "rt_exp", "member_ready", "rank_ps", "routed", "acc_ready",
        "pick_ready", "pickT_ps", "pickT_sb", "comb_ps", "comb_sb", "gath_ps", "gath_sb",
        "guA_ps", "guB_ps", "silu_a", "silu_b", "hid_a", "hid_b", "hidT_ps", "hidTa_sb", "hidTb_sb",
        "y_ps", "y_act", "y_dve", "x_act", "x_dve", "out_ready", "out_landed")}

    gate_d = w_gate.rearrange("l g e (p k) f -> (l g e) p (k f)", k=KD)
    up_d = w_up.rearrange("l g e (p k) f -> (l g e) p (k f)", k=KD)
    down_d = w_down.rearrange("l g e (j p) n -> (l g e) p j n", p=P)
    win_d = w_in.rearrange("l (p k) n -> l p k n", k=KD)
    wout_d = w_out.rearrange("l (m j p) n -> l m p j n", j=2, p=P)
    wuq_d = w_uq.rearrange("l (c p) n -> l p c n", p=P)
    wukv_d = w_ukv.rearrange("l (c p) n -> l p c n", p=P)
    x_d = x_in.rearrange("b (t p) d -> p (b t) d", p=P)
    out_d = out.rearrange("b (t p) d -> p (b t) d", p=P)

    def dyn(ap, i):
        return ap[bass.ds(i, 1)].rearrange("a p n -> (a p) n") if len(ap.shape) == 3 else \
            ap[bass.ds(i, 1)].rearrange("a p j n -> (a p) j n")

    def wslot(n, j=2):
        return ring[:, n, 0:2048].rearrange("p (j n) -> p j n", j=j)

    def col(tensor, l):
        return tensor[:, bass.ds(l, 1)]

    def lay(tensor, l):
        return tensor[:, bass.ds(l, 1), :].rearrange("p a n -> p (a n)")

    def past(eng):
        eng.sem_inc(s["passed"], 1)

    def load_npass(eng, l):
        eng.wait_ge(s["routed"], l + 1)
        past(eng)
        return eng.value_load(npass_t[0:1, 0:1], min_val=1, max_val=T // SLOTS)

    WOUT_SLOT = (12, 13, 8, 9)

    def wout_part(l, m):
        return wout_d[bass.ds(l, 1), m].rearrange("a p j n -> (a p) j n")

    IN_JOBS = [(0, 0, C_Q), (1, 1, C_Q), (2, 0, C_KV), (3, 1, C_KV), (4, 0, C_SQK), (5, 1, C_SQK),
               (6, 0, C_VDQ), (7, 1, C_VDQ), (0, 0, C_DKV), (1, 1, C_DKV)]
    UQ_JOBS = [(5, 0, 0), (6, 0, 1), (7, 1, 0), (0, 1, 1)]
    UKV_JOBS = [(1, 0, 0), (2, 0, 1), (3, 1, 0), (4, 1, 1)]
    T_BANKS = [5, 6, 7, 0, 1, 2, 3, 4, 5, 6]

    def maps():
        for h in range(MLA_H):
            yield (lambda qt, h=h: qTm[0:MLA_QK, h, qt * P:(qt + 1) * P], kTm[0:MLA_QK, h, :],
                   lambda kt, h=h: vm[:, kt, h * MLA_V:(h + 1) * MLA_V], h * MLA_V, "mla", h)
        for h in range(SWA_H):
            c, b = h % 3, h // 3
            yield (lambda qt, c=c: qTs[:, c, qt * P:(qt + 1) * P], kps[:, b, :],
                   lambda kt, b=b: vsd[:, kt, b * HD:(b + 1) * HD], MLA_H * MLA_V + h * HD, "swa", h)
        for m in range(2 * DIFF_H):
            h = m // 2
            yield (lambda qt, m=m: qTd[:, m // 4, qt * P:(qt + 1) * P], kpd[:, m, :],
                   lambda kt, h=h: vsd[:, kt, SWA_KV * HD + h * DV:SWA_KV * HD + (h + 1) * DV],
                   (MLA_H + SWA_H) * HD + h * DV, "diff", m)

    MAPS = list(maps())
    NPLAIN = MLA_H + SWA_H
    NUNITS = NPLAIN + DIFF_H
    GROUPS = [(n, n + 1) for n in range(0, NPLAIN, 2)] + [(n,) for n in range(NPLAIN, NUNITS)]
    TURNED = ("probT_act", "probT_dve")

    def unit_of(m):
        return m if m < NPLAIN else NPLAIN + (m - NPLAIN) // 2

    def last_map(n):
        return n if n < NPLAIN else NPLAIN + 2 * (n - NPLAIN) + 1

    def unit_buf(n):
        return (n if n < NPLAIN else last_map(n) - 1) % 4

    def unit_at(m):
        return next((n for n in range(NUNITS) if last_map(n) == m), None)

    def group_of(n):
        return next(g for g, units in enumerate(GROUPS) if n in units)

    def group_at(m):
        return next((g for g, units in enumerate(GROUPS) if last_map(units[-1]) == m), None)

    with nc.Block() as block:

        @block.sync
        def _(sp):
            passes = sp.alloc_register("sp_passes")
            sp.reg_mov(passes, 0)
            sp.dma_start(x[:, :, :], x_d).then_inc(s["x_landed"], 16)
            sp.wait_ge(s["const_landed"], 16)
            def pass_loads(l, p_before):
                with sp.Fori(0, NIT) as i:
                    n = l + 1 + p_before * NIT + i
                    e = l * NE + 4 * i
                    sp.wait_ge(s["freed_a"], n + 1)
                    for m, ex in ((0, 0), (2, 2)):
                        sp.dma_start(ring[:, m, 0:2048], dyn(gate_d, e + ex)).then_inc(s["landed_a"], 16)
                        sp.dma_start(ring[:, m + 1, 0:2048], dyn(up_d, e + ex)).then_inc(s["landed_a"], 16)
                    sp.wait_ge(s["freed_b"], n + 1)
                    for m, ex in ((4, 1), (6, 3)):
                        sp.dma_start(ring[:, m, 0:2048], dyn(gate_d, e + ex)).then_inc(s["landed_b"], 16)
                        sp.dma_start(ring[:, m + 1, 0:2048], dyn(up_d, e + ex)).then_inc(s["landed_b"], 16)
                    sp.wait_ge(s["freed_da"], n + 1)
                    for m, ex in ((8, 0), (9, 2)):
                        sp.dma_start(wslot(m), dyn(down_d, e + ex)).then_inc(s["landed_da"], 16)
                    sp.wait_ge(s["freed_db"], p_before * NIT + i + 1)
                    for m, ex in ((10, 1), (11, 3)):
                        sp.dma_start(wslot(m), dyn(down_d, e + ex)).then_inc(s["landed_db"], 16)

            with sp.Fori(0, L) as l:
                before = sp.snap(passes)
                n = l + before * NIT
                for name, k0 in (("a", 0), ("b", 4)):
                    sp.wait_ge(s["freed_" + name], n + 1)
                    for k in range(k0, k0 + 4):
                        src = win_d[bass.ds(l, 1), :, k, :].rearrange("a p n -> (a p) n")
                        sp.dma_start(ring[:, k, :], src).then_inc(s["landed_" + name], 16)
                sp.wait_ge(s["freed_up"], 2 * l + 1)
                sp.dma_start(ring[:, 12, 0:3 * 576].rearrange("p (c n) -> p c n", c=3), dyn(wuq_d, l)).then_inc(s["landed_uq"], 16)
                sp.dma_start(ring[:, 13, 0:2 * 768].rearrange("p (c n) -> p c n", c=2), dyn(wukv_d, l)).then_inc(s["landed_ukv"], 16)
                sp.wait_ge(s["freed_da"], n + 1)
                for m in (2, 3):
                    sp.dma_start(wslot(WOUT_SLOT[m]), wout_part(l, m)).then_inc(s["landed_da"], 16)
                sp.wait_ge(s["freed_up"], 2 * l + 2)
                past(sp)
                for m in (0, 1):
                    sp.dma_start(wslot(WOUT_SLOT[m]), wout_part(l, m)).then_inc(s["landed_wo"], 16)
                pass_loads(l, before)
                sp.reg_add(passes, passes, 1)
                npass = load_npass(sp, l)
                with sp.If(npass > 1):
                    with sp.Fori(1, npass):
                        pass_loads(l, sp.snap(passes))
                        sp.reg_add(passes, passes, 1)
            sp.wait_ge(s["out_ready"], 2)
            sp.dma_start(out_d, hT[:, :, :].rearrange("p (t k) n -> p t (k n)", t=TT)).then_inc(s["out_landed"], 16)
            sp.wait_ge(s["out_landed"], 16)

        @block.tensor
        def _(pe):
            passes = pe.alloc_register("pe_passes")
            pe.reg_mov(passes, 0)
            for n in ("freed_a", "freed_b", "freed_da", "freed_db", "freed_up"):
                pe.sem_inc(s[n], 1)

            def turn_h(l, which):
                pe.wait_ge(s["h_act"], 2 * l + which + 1)
                pe.wait_ge(s["h_dve"], 2 * l + which + 1)
                for b in range(4):
                    for c in range(4):
                        k, tt = 2 * b + c // 2, c % 2
                        t = pe.transpose(ps[:, b, c * P:(c + 1) * P], hA[:, tt, k, :], ident)
                        if which == 1 and b == 0 and c < 2:
                            t.then_inc(s["freed_da" if c == 0 else "freed_up"], 1)
                    t.then_inc(s["hT_ps"], 1)

            def prepare(q, free_b=True):
                pe.wait_ge(s["pick_ready"], q + 1)
                for tt in range(TT):
                    mm = pe.matmul(ps[:, 6, 0:4], pick[:, tt, :], comb[:, tt, bass.ds(q_pair[0], 4)],
                                   start=(tt == 0), stop=(tt == TT - 1))
                    if tt == 0 and free_b:
                        mm.then_inc(s["freed_b"], 1)
                mm.then_inc(s["comb_ps"], 1)
                for bank, k0 in ((5, 0), (4, 4)):
                    for k in range(k0, k0 + 4):
                        for tt in range(TT):
                            mm = pe.matmul(ps[:, bank, (k - k0) * P:(k - k0 + 1) * P], hA[:, tt, k, :], pick[:, tt, :],
                                           start=(tt == 0), stop=(tt == TT - 1))
                    mm.then_inc(s["gath_ps"], 1)

            q_pair = [0]
            with pe.Fori(0, L) as l:
                before = pe.snap(passes)
                n = l + before * NIT
                if True:
                    pe.wait_ge(s["const_landed"], 16)
                    turn_h(l, 0)
                    pe.wait_ge(s["hT_sb"], 8 * l + 4)
                    pe.wait_ge(s["landed_a"], 64 * n + 64)
                    pe.wait_ge(s["landed_b"], 64 * n + 64)
                    for j, (bank, tt, (c0, w)) in enumerate(IN_JOBS):
                        if j in (8, 9):
                            pe.wait_ge(s["low_ready"], 4 * l + j - 7)
                        for k in range(KD):
                            mm = pe.matmul(ps[:, bank, 0:w], hT[:, k, tt * P:(tt + 1) * P], ring[:, k, c0:c0 + w],
                                           start=(k == 0), stop=(k == KD - 1))
                        mm.then_inc(s["u_ps"], 1)
                    pe.wait_ge(s["low_ready"], 4 * l + 4)
                    for c in range(5):
                        bank = 2 + c // 2
                        if c == 0:
                            pe.wait_ge(s["rope_mul"], 12 * l + 2)
                        if c == 4:
                            pe.wait_ge(s["rope_mul"], 12 * l + 3)
                        for tt in range(TT):
                            t = pe.transpose(ps[:, bank, (c % 2) * T + tt * P:(c % 2) * T + (tt + 1) * P],
                                             low[:, tt, c * P:(c + 1) * P], ident)
                            if c == 0:
                                t.then_inc(s["freed_a" if tt == 0 else "freed_b"], 1)
                        if c in (1, 3, 4):
                            t.then_inc(s["lowT_ps"], 1)
                    pe.wait_ge(s["lowT_sb"], 3 * l + 3)
                    pe.wait_ge(s["landed_uq"], 16 * l + 16)
                    pe.wait_ge(s["landed_ukv"], 16 * l + 16)
                    wq = ring[:, 12, 0:3 * 576].rearrange("p (c n) -> p c n", c=3)
                    wkv = ring[:, 13, 0:2 * 768].rearrange("p (c n) -> p c n", c=2)
                    for j, (bank, tt, half) in enumerate(UQ_JOBS):
                        pe.wait_ge(s["rope_mul"], 12 * l + 4 + j)
                        for c in range(3):
                            mm = pe.matmul(ps[:, bank, 0:288], lowT[:, c, tt * P:(tt + 1) * P],
                                           wq[:, c, half * 288:(half + 1) * 288], start=(c == 0), stop=(c == 2))
                        mm.then_inc(s["up_ps"], 1)
                    pe.wait_ge(s["rope_mul"], 12 * l + 8)
                    for j, (bank, tt, half) in enumerate(UKV_JOBS):
                        for c in range(2):
                            mm = pe.matmul(ps[:, bank, 0:384], lowT[:, 3 + c, tt * P:(tt + 1) * P],
                                           wkv[:, c, half * 384:(half + 1) * 384], start=(c == 0), stop=(c == 1))
                        mm.then_inc(s["up_ps"], 1)
                    pe.wait_ge(s["rope_add"], 12 * l + 8)
                    for j in range(4):
                        pe.wait_ge(s["rope_mul"], 12 * l + 9 + j)
                        for c in (2 * j, 2 * j + 1):
                            for tt in range(TT):
                                t = pe.transpose(ps[:, T_BANKS[j], (c % 2) * T + tt * P:(c % 2) * T + (tt + 1) * P],
                                                 rq[:, tt, c * P:(c + 1) * P], ident)
                                if c == 0 and tt == 0:
                                    t.then_inc(s["freed_up"], 1)
                        t.then_inc(s["T_ps"], 1)
                    pe.wait_ge(s["rope_add"], 12 * l + 12)
                    pe.wait_ge(s["kv_sb"], 4 * l + 4)
                    pe.wait_ge(s["krope_sb"], l + 1)
                    for j in range(4, 10):
                        if j == 8:
                            pe.wait_ge(s["T_act"], 5 * l + 1)
                            pe.wait_ge(s["T_dve"], 5 * l + 1)
                        src = qm if j < 7 else km
                        for hh in range(2):
                            h = 2 * ((j - 4) % 3) + hh
                            for tt in range(TT):
                                t = pe.transpose(ps[0:MLA_QK, T_BANKS[j], hh * T + tt * P:hh * T + (tt + 1) * P],
                                                 src[:, tt, h, :], ident)
                        t.then_inc(s["T_ps"], 1)
                    pe.wait_ge(s["T_act"], 5 * l + 5)
                    pe.wait_ge(s["T_dve"], 5 * l + 5)
                    for t_ in range(NMAPS + 5):
                        if t_ < NMAPS:
                            q_of, k_all = MAPS[t_][0:2]
                            if t_ >= 3:
                                pe.wait_ge(s["prob_ready"], NMAPS * l + t_ - 2)
                            for qt in range(TT):
                                mm = pe.matmul(ps[:, t_ % 3, qt * T:(qt + 1) * T], q_of(qt), k_all, start=True, stop=True)
                            mm.then_inc(s["score_ps"], 1)
                        n_ = unit_at(t_ - 3)
                        if n_ is not None:
                            pe.wait_ge(s["scaled"], NUNITS * l + n_ + 1)
                            if n_ >= 2:
                                pe.wait_ge(s[TURNED[n_ % 2]], (NUNITS // 2) * l + n_ // 2)
                            for kt in range(TT):
                                for qt in range(TT):
                                    t = pe.transpose(ps[:, 3 + n_ % 2, kt * T + qt * P:kt * T + (qt + 1) * P],
                                                     prob[unit_buf(n_)][:, qt, kt * P:(kt + 1) * P], ident)
                            t.then_inc(s["probT_ps"], 1)
                        g_ = group_at(t_ - 4)
                        if g_ is None:
                            continue
                        units = GROUPS[g_]
                        for n_ in units:
                            pe.wait_ge(s[TURNED[n_ % 2]], (NUNITS // 2) * l + n_ // 2 + 1)
                        if g_ >= 2:
                            pe.wait_ge(s["o_sb"], len(GROUPS) * l + g_ - 1)
                        bank = 5 + g_ % 2
                        if len(units) == 2:
                            for kt in range(TT):
                                for w, n_ in enumerate(units):
                                    mm = pe.matmul(ps[64 * w:64 * w + 64, bank, 0:T], MAPS[n_][2](kt),
                                                   probT[n_ % 4][:, kt, :], start=(kt == 0), stop=(kt == TT - 1))
                        else:
                            n_, = units
                            v_of = MAPS[NPLAIN + 2 * (n_ - NPLAIN)][2]
                            for qt in range(TT):
                                for kt in range(TT):
                                    mm = pe.matmul(ps[:, bank, qt * DV:(qt + 1) * DV], probT[n_ % 4][:, kt, qt * P:(qt + 1) * P],
                                                   v_of(kt), start=(kt == 0), stop=(kt == TT - 1))
                        mm.then_inc(s["o_ps"], 1)
                    pe.wait_ge(s["o_sb"], len(GROUPS) * l + len(GROUPS) - DIFF_H)
                    pe.wait_ge(s[TURNED[0]], (NUNITS // 2) * l + NUNITS // 2)
                    pe.wait_ge(s[TURNED[1]], (NUNITS // 2) * l + NUNITS // 2)
                    pe.wait_ge(s["o_sb"], len(GROUPS) * l + len(GROUPS))
                    pe.wait_ge(s["landed_da"], 32 * n + 32)
                    pe.wait_ge(s["landed_wo"], 32 * l + 32)

                    def project(tt, half, ks):
                        for k in ks:
                            mm = pe.matmul(ps[:, 4 + 2 * tt + half, :], hT[:, k, tt * P:(tt + 1) * P],
                                           wslot(WOUT_SLOT[k // 2])[:, k % 2, half * 512:(half + 1) * 512],
                                           start=(k == 0), stop=(k == KD - 1))
                        return mm

                    project(0, 0, range(6))
                    pe.wait_ge(s["dnorm_ready"], l + 1)
                    for c in range(2):
                        for tt in range(TT):
                            t = pe.transpose(ps[:, 0, c * T + tt * P:c * T + (tt + 1) * P], odiff[:, tt, c * P:(c + 1) * P], ident)
                    t.then_inc(s["oT_ps"], 1)
                    for j in range(4):
                        if j == 0:
                            project(0, 1, range(6))
                            pe.wait_ge(s["oT_dve"], l + 1)
                        tt, half = j // 2, j % 2
                        project(tt, half, range(6, KD) if j < 2 else range(KD)).then_inc(s["wout_ps"], 1)
                turn_h(l, 1)
                pe.wait_ge(s["hT_sb"], 8 * l + 8)
                for k in range(KD):
                    mm = pe.matmul(ps[0:G + NE, 4, 0:T], w_rl[:, k, :], hT[:, k, :], start=(k == 0), stop=(k == KD - 1))
                mm.then_inc(s["logitT_ps"], 1)
                pe.wait_ge(s["logitT_sb"], l + 1)
                past(pe)
                for tt in range(TT):
                    t = pe.transpose(ps[:, 4, tt * 64:tt * 64 + G + NE], logitT[:, tt * P:(tt + 1) * P], ident[0:G + NE, 0:G + NE])
                t.then_inc(s["logit_ps"], 1)
                for tt in range(TT):
                    for half in range(2):
                        mm = pe.matmul(ps[:, 2 * tt + half, :], ident, x[:, tt, half * 512:(half + 1) * 512],
                                       start=True, stop=False, skip_group_check=True)
                pe.wait_ge(s["member_ready"], l + 1)
                pe.matmul(ps[:, 5, 0:16], tri, member[:, 0, :], start=True, stop=True)
                pe.matmul(ps[:, 5, 32:48], ones, member[:, 0, :], start=True, stop=False)
                pe.matmul(ps[:, 5, 32:48], tri, member[:, 1, :], start=False, stop=True)
                pe.matmul(ps[:, 5, 64:80], ones, member[:, 0, :], start=True, stop=False)
                pe.matmul(ps[:, 5, 64:80], ones, member[:, 1, :], start=False, stop=True).then_inc(s["rank_ps"], 1)
                npass = load_npass(pe, l)
                with pe.Fori(0, npass):
                    done = pe.snap(passes)
                    q_pair[0] = 0
                    prepare(done * (NIT + 1), False)
                    with pe.Fori(0, NIT) as i:
                        u = done * NIT + i
                        q = done * (NIT + 1) + i
                        use = l + 1 + u
                        pe.wait_ge(s["gath_sb"], 2 * q + 2)
                        for tt in range(TT):
                            t = pe.transpose(ps[:, 4, tt * P:(tt + 1) * P], pick[:, tt, :], ident)
                        t.then_inc(s["pickT_ps"], 1)
                        for which, (slot, land, bank) in enumerate(((0, "landed_a", 6), (4, "landed_b", 7))):
                            pe.wait_ge(s[land], 64 * use + 64)
                            if which == 0:
                                pe.wait_ge(s["comb_sb"], q + 1)
                            for k in range(KD):
                                for pr in range(2):
                                    mm = pe.matmul(ps[64 * pr:64 * pr + 64, bank, :].rearrange("p (w f) -> p w f", w=2),
                                                   hTg[:, k, 64 * pr:64 * pr + 64],
                                                   ring[:, slot + 2 * pr:slot + 2 * pr + 2, k * F:(k + 1) * F],
                                                   start=(k == 0), stop=(k == KD - 1))
                                    if which == 1 and k == 0 and pr == 0:
                                        mm.then_inc(s["freed_a"], 1)
                            mm.then_inc(s["guA_ps" if which == 0 else "guB_ps"], 1)
                        pe.wait_ge(s["pickT_sb"], u + 1)
                        pe.wait_ge(s["hid_a"], u + 1)
                        q_pair[0] = 4 * i + 4
                        prepare(q + 1)
                        pe.wait_ge(s["comb_sb"], q + 2)
                        for which in range(2):
                            if which == 1:
                                pe.wait_ge(s["hid_b"], u + 1)
                            for j in range(2):
                                t = pe.transpose(ps[:, 6 + which, j * P:(j + 1) * P], hid[which][:, j * P:(j + 1) * P], ident)
                            t.then_inc(s["hidT_ps"], 1)
                        pe.wait_ge(s["gath_sb"], 2 * q + 4)
                        for which, (slot, land) in enumerate(((8, "landed_da"), (10, "landed_db"))):
                            pe.wait_ge(s[land], 32 * (use if which == 0 else u) + 32)
                            pe.wait_ge(s["hidTa_sb" if which == 0 else "hidTb_sb"], u + 1)
                            for half in range(2):
                                for j in range(2):
                                    for pr in range(2):
                                        mm = pe.matmul(ps[64 * pr:64 * pr + 64, 4 + half, :],
                                                       hidT[which][:, j, 64 * pr:64 * pr + 64],
                                                       wslot(slot + pr)[:, j, half * 512:(half + 1) * 512],
                                                       start=(which == 0 and j == 0), stop=(which == 1 and j == 1),
                                                       skip_group_check=True)
                            mm.then_inc(s["freed_da" if which == 0 else "y_ps"], 1)
                        pe.wait_ge(s["y_act"], u + 1)
                        pe.wait_ge(s["y_dve"], u + 1)
                        for tt in range(TT):
                            for half in range(2):
                                mm = pe.matmul(ps[:, 2 * tt + half, :], pickT[:, tt * P:(tt + 1) * P], y_sb[:, half, :],
                                               start=False, stop=False, skip_group_check=True)
                                if tt == 0 and half == 0:
                                    mm.then_inc(s["freed_db"], 1)
                        mm.then_inc(s["acc_ready"], 1)
                    pe.reg_add(passes, passes, 1)

        @block.scalar
        def _(act):
            passes = act.alloc_register("act_passes")
            act.reg_mov(passes, 0)

            def norm_rows(l, which):
                act.activation(hAf[:, 0:D], x[:, 0, :], ACT.Square, accum_out=ssq[:, 0:1]).then_inc(s["sq_act"], 1)
                act.wait_ge(s["rms_ready"], 2 * l + which + 1)
                act.activation(hA[:, 0, :, :], x[:, 0, :].rearrange("p (j k) -> p k j", k=KD), ACT.Copy,
                               scale=rs[:, 0:1]).then_inc(s["h_act"], 1)

            first = [
                (g_attn[:, :, :], attn_norm.rearrange("l (p k) -> p l k", k=KD)),
                (sink[:, :, :], swa_sink.rearrange("(a l) n -> a l n", a=1).broadcast_to([P, L, SWA_H])),
                (subln[0:64, :], diff_subln.rearrange("l p -> p l")),
                (subln[64:128, :], diff_subln.rearrange("l p -> p l")),
            ]
            first += [(lqk[:, n, :, :], v.rearrange("(a l) n -> a l n", a=1).broadcast_to([P, L, DQK]))
                      for n, v in enumerate((lq1, lk1, lq2, lk2))]
            for l in range(L):
                first += [(g_low[:, l, 0:3], mla_q_norm[l].rearrange("(c p) -> p c", p=P)),
                          (g_low[:, l, 3:5], mla_kv_norm[l].rearrange("(c p) -> p c", p=P))]
            second = [
                (g_ffn[:, :, :], ffn_norm.rearrange("l (p k) -> p l k", k=KD)),
                (rbias[:, :, 0:G], router_group_bias.rearrange("(a l) n -> a l n", a=1).broadcast_to([P, L, G])),
                (rbias[:, :, G:G + NE], router_expert_bias.rearrange("(a l) n -> a l n", a=1).broadcast_to([P, L, NE])),
            ]
            for l in range(L):
                second += [(w_r[:, l, :, 0:G], router_group[l].rearrange("(p k) g -> p k g", k=KD)),
                           (w_r[:, l, :, G:G + NE], router_expert[l].rearrange("(p k) g -> p k g", k=KD))]
            second.append((g_fin[:, :], final_norm.rearrange("(a n) -> a n", a=1).broadcast_to([P, D])))
            assert len(first) == N_FIRST and len(second) == N_SECOND
            act.dma_start(cst[:, :], const).then_inc(s["const_landed"], 16)
            with nc.allow_non_contiguous_dma("small parameters"):
                for dst, src in first:
                    act.dma_start(dst, src).then_inc(s["params_landed"], 16)
                act.wait_ge(s["landed_b"], 64)
                for dst, src in second:
                    act.dma_start(dst, src).then_inc(s["router_landed"], 16)
            act.wait_ge(s["x_landed"], 16)
            act.wait_ge(s["cleared"], 2)
            with act.Fori(0, L) as l:
                norm_rows(l, 0)
                act.wait_ge(s["lam_sum"], l + 1)
                act.activation(lam[:, 2:4], lam[:, 0:2], ACT.Exp).then_inc(s["lam_exp"], 1)
                for j in range(4):
                    w, c0 = (MLA_QR, 0) if j < 2 else (MLA_KVR, MLA_QR)
                    act.wait_ge(s["u_ps"], 10 * l + j + 1)
                    act.activation(msf[:, 0:w], ps[:, j, 0:w], ACT.Square, accum_out=ssc[:, j:j + 1]).then_inc(s["low_sq"], 1)
                    act.drain()
                for j in range(4):
                    w, c0 = (MLA_QR, 0) if j < 2 else (MLA_KVR, MLA_QR)
                    act.wait_ge(s["low_rms"], 2 * l + 1 + j // 2)
                    act.activation(low[:, j % 2, c0:c0 + w], ps[:, j, 0:w], ACT.Copy,
                                   scale=rsc[:, j:j + 1]).then_inc(s["low_ready"], 1)
                for j in range(6, 10):
                    act.wait_ge(s["u_ps"], 10 * l + j + 1)
                    bank, tt = IN_JOBS[j][0:2]
                    if j < 8:
                        act.copy(vsd[:, tt, 0:128], ps[:, bank, 0:128]).then_inc(s["v_sb"], 1)
                    else:
                        act.copy(vsd[:, tt, 128:384], ps[:, bank, 256:512]).then_inc(s["v_sb"], 1)
                for j, (bank, tt, half) in enumerate(UQ_JOBS):
                    act.wait_ge(s["up_ps"], 8 * l + j + 1)
                    v = ps[:, bank, 0:288].rearrange("p (h d) -> p h d", h=3)
                    act.copy(qm[:, tt, 3 * half:3 * half + 3, 0:NOPE], v[:, :, 0:NOPE]).then_inc(s["q_nope"], 1)
                for j, (bank, tt, half) in enumerate(UKV_JOBS):
                    act.wait_ge(s["up_ps"], 8 * l + j + 5)
                    v = ps[:, bank, 0:384].rearrange("p (h d) -> p h d", h=3)
                    act.copy(km[:, tt, 3 * half:3 * half + 3, 0:NOPE], v[:, :, 0:NOPE])
                    act.copy(vm[:, tt, 192 * half:192 * half + 192].rearrange("p (h d) -> p h d", h=3),
                             v[:, :, NOPE:128]).then_inc(s["kv_sb"], 1)
                for j in (0, 2, 4, 6, 8):
                    act.wait_ge(s["T_ps"], 10 * l + j + 1)
                    v = ps[:, T_BANKS[j], :].rearrange("p (c t) -> p c t", c=2)
                    if j == 0:
                        i = act.activation(qTs[:, 0:2, :], v, ACT.Copy, scale=HD ** -0.5)
                    elif j == 2:
                        i = act.activation(qTd[:, :, :], v, ACT.Copy, scale=DQK ** -0.5)
                    elif j < 7:
                        i = act.activation(qTm[0:MLA_QK, 2 * (j - 4):2 * (j - 4) + 2, :], v[0:MLA_QK], ACT.Copy,
                                           scale=MLA_QK ** -0.5)
                    else:
                        i = act.copy(kTm[0:MLA_QK, 2 * (j - 7):2 * (j - 7) + 2, :], v[0:MLA_QK])
                    i.then_inc(s["T_act"], 1)
                for t_ in range(NMAPS + 3):
                    if t_ < NMAPS:
                        kind, n = MAPS[t_][4:6]
                        act.wait_ge(s["nmax_ready"], NMAPS * l + t_ + 1)
                        if t_ >= 4:
                            act.wait_ge(s["probT_ps"], NUNITS * l + unit_of(t_ - 4) + 1)
                        if kind == "swa":
                            act.activation(esink[:, n, :], nmax[:, t_, :], ACT.Exp,
                                           bias=sink[:, bass.ds(l, 1), n:n + 1].rearrange("p a n -> p (a n)"))
                        for qt in range(TT):
                            src = ms[:, qt, :] if kind == "swa" else ps[:, t_ % 3, qt * T:(qt + 1) * T]
                            i = act.activation(prob[t_ % 4][:, qt, :], src, ACT.Exp, bias=nmax[:, t_, qt:qt + 1],
                                               accum_out=psum_[:, t_, qt:qt + 1])
                        i.then_inc(s["prob_ready"], 1)
                    m = unit_at(t_ - 3)
                    if m is not None and m % 2 == 0:
                        act.wait_ge(s["probT_ps"], NUNITS * l + m + 1)
                        if m >= 4:
                            act.wait_ge(s["o_ps"], len(GROUPS) * l + group_of(m - 4) + 1)
                        act.copy(probT[m % 4], ps[:, 3, :].rearrange("p (k t) -> p k t", k=TT)).then_inc(s[TURNED[0]], 1)
                act.wait_ge(s["x_mixed"], 4 * l + 2)
                norm_rows(l, 1)
                act.wait_ge(s["rt_dve"], 2 * l + 1)
                for tt in range(TT):
                    i = act.activation(gexp[:, tt, :], gl8[:, tt, 0:G], ACT.Exp, bias=ngm[:, tt:tt + 1],
                                       accum_out=gsum[:, tt:tt + 1])
                i.then_inc(s["rt_exp"], 1)
                act.wait_ge(s["rt_dve"], 2 * l + 2)
                act.activation(wts[:, 1, :], wts[:, 0, :], ACT.Exp).then_inc(s["rt_exp"], 1)
                npass = load_npass(act, l)
                with act.Fori(0, npass):
                    done = act.snap(passes)
                    with act.Fori(0, NIT) as i:
                        u = done * NIT + i
                        act.wait_ge(s["pickT_ps"], u + 1)
                        act.copy(pickT, ps[:, 4, 0:T]).then_inc(s["pickT_sb"], 1)
                        act.wait_ge(s["guA_ps"], u + 1)
                        act.activation(sil[0], ps[:, 6, 0:F], ACT.Silu).then_inc(s["silu_a"], 1)
                        act.wait_ge(s["guB_ps"], u + 1)
                        act.activation(sil[1], ps[:, 7, 0:F], ACT.Silu).then_inc(s["silu_b"], 1)
                        act.wait_ge(s["hidT_ps"], 2 * u + 1)
                        act.copy(hidT[0], ps[:, 6, 0:T].rearrange("p (j s) -> p j s", j=2)).then_inc(s["hidTa_sb"], 1)
                        act.wait_ge(s["y_ps"], u + 1)
                        act.copy(y_sb[:, 1, :], ps[:, 5, :]).then_inc(s["y_act"], 1)
                    act.reg_add(passes, passes, 1)
                act.wait_ge(s["acc_ready"], act.snap(passes) * NIT)
                act.copy(x[:, 0, :].rearrange("p (b n) -> p b n", b=2), ps[:, 0:2, :]).then_inc(s["x_act"], 1)
                act.drain()
            act.activation(hAf[:, 0:D], x[:, 0, :], ACT.Square, accum_out=ssq[:, 0:1]).then_inc(s["sq_act"], 1)

        @block.gpsimd
        def _(pool):
            pool.memset(nhalf[:, :], -0.5).then_inc(s["cleared"], 1)
            pool.drain()

            def rms(out_, in_, width, n, sem):
                past(pool)
                pool.tensor_scalar(out_, in_, 1.0 / width, EPS, ALU.mult, ALU.add)
                pool.drain()
                pool.tensor_tensor(out_, out_, nhalf[:, 0:n], ALU.pow).then_inc(sem, 1)
                pool.drain()

            def add(out_, r, w, shape=None):
                a, b = tmpA[r % 2][:, 0:w], tmpB[r % 2][:, 0:w]
                return pool.tensor_tensor(out_, shape(a) if shape else a, shape(b) if shape else b, ALU.add)

            with pool.Fori(0, L) as l:
                pool.wait_ge(s["sq_act"], 2 * l + 1)
                pool.wait_ge(s["sq_dve"], 2 * l + 1)
                rms(rs[:, :], ssq[:, :], D, TT, s["rms_ready"])
                for half, w in ((0, MLA_QR), (1, MLA_KVR)):
                    pool.wait_ge(s["low_sq"], 4 * l + 2 * half + 2)
                    rms(rsc[:, 2 * half:2 * half + 2], ssc[:, 2 * half:2 * half + 2], w, 2, s["low_rms"])
                heads = lambda n: (lambda v: v.rearrange("p (h d) -> p h d", h=n))
                for r in range(12):
                    pool.wait_ge(s["rope_mul"], 12 * l + r + 1)
                    tt = r % 2
                    if r < 2:
                        i = add(kro[:, tt, :], r, ROPE)
                    elif r < 4:
                        a, b = tmpA[tt][:, 0:384], tmpB[tt][:, 0:384]
                        f = lambda v: v.rearrange("p (b c d) -> p b c d", b=2, c=3)
                        pool.tensor_tensor(rq[:, tt, 0:384].rearrange("p (c b d) -> p b c d", b=2, c=3), f(a), f(b), ALU.add)
                        i = pool.tensor_tensor(rq[:, tt, 384:512], tmpA[tt][:, 384:512], tmpB[tt][:, 384:512], ALU.add)
                    elif r < 8:
                        c0 = 512 if r < 6 else 768
                        i = add(rq[:, tt, c0:c0 + 256], r, 256)
                    else:
                        _, t2, half = UQ_JOBS[r - 8]
                        i = add(qm[:, t2, 3 * half:3 * half + 3, NOPE:MLA_QK], r, 3 * ROPE, heads(3))
                    i.then_inc(s["rope_add"], 1)
                    if r == 1:
                        pool.drain()
                    if r == 7:
                        for t2 in range(TT):
                            i = pool.tensor_copy(km[:, t2, :, NOPE:MLA_QK],
                                                 kro[:, t2, :].unsqueeze(1).broadcast_to([P, MLA_H, ROPE]))
                        i.then_inc(s["krope_sb"], 1)
                pool.wait_ge(s["dsq_ready"], l + 1)
                rms(drs[:, :], dssq[:, :], DV, 8, s["drms_ready"])
                pool.wait_ge(s["sq_act"], 2 * l + 2)
                pool.wait_ge(s["sq_dve"], 2 * l + 2)
                rms(rs[:, :], ssq[:, :], D, TT, s["rms_ready"])
            pool.wait_ge(s["sq_act"], 2 * L + 1)
            pool.wait_ge(s["sq_dve"], 2 * L + 1)
            rms(rs[:, :], ssq[:, :], D, TT, s["rms_ready"])

        @block.vector
        def _(dve):
            passes = dve.alloc_register("dve_passes")
            dve.reg_mov(passes, 0)

            def norm_rows(l, which):
                dve.tensor_tensor_reduce(hAf[:, D:2 * D], x[:, 1, :], x[:, 1, :], 1.0, 0.0, ALU.mult, ALU.add,
                                         ssq[:, 1:2]).then_inc(s["sq_dve"], 1)
                dve.wait_ge(s["rms_ready"], 2 * l + which + 1)
                dve.tensor_scalar(hA[:, 1, :, :], x[:, 1, :].rearrange("p (j k) -> p k j", k=KD), rs[:, 1:2], None,
                                  ALU.mult).then_inc(s["h_dve"], 1)

            def turn_out(l, which, gain):
                g = lay(gain, l)
                for b in range(4):
                    dve.wait_ge(s["hT_ps"], 8 * l + 4 * which + b + 1)
                    dve.tensor_tensor(hT[:, 2 * b:2 * b + 2, :], ps[:, b, :].rearrange("p (c t) -> p c t", c=2),
                                      g[:, 2 * b:2 * b + 2].unsqueeze(2).broadcast_to([P, 2, T]), ALU.mult).then_inc(s["hT_sb"], 1)

            def rope(l, r, tt, src, nh, dim):
                h = dim // 2
                if r >= 2:
                    dve.wait_ge(s["rope_add"], 12 * l + r - 1)
                a, b = tmpA[r % 2][:, 0:nh * dim], tmpB[r % 2][:, 0:nh * dim]
                cos, sin, nsin = (table(dim, n, tt) for n in range(3))
                dve.tensor_tensor(a.rearrange("p (h d) -> p h d", d=h) if len(src.shape) == 2 else
                                  a.rearrange("p (h w d) -> p h w d", w=2, d=h),
                                  src.rearrange("p (h d) -> p h d", d=h) if len(src.shape) == 2 else
                                  src.rearrange("p h (w d) -> p h w d", w=2),
                                  cos.unsqueeze(1).broadcast_to([P, 2 * nh, h]) if len(src.shape) == 2 else
                                  cos.unsqueeze(1).unsqueeze(1).broadcast_to([P, nh, 2, h]), ALU.mult)
                bv = b.rearrange("p (h w d) -> p h w d", w=2, d=h)
                sv = src.rearrange("p (h w d) -> p h w d", w=2, d=h) if len(src.shape) == 2 else \
                    src.rearrange("p h (w d) -> p h w d", w=2)
                dve.tensor_tensor(bv[:, :, 0, :], sv[:, :, 1, :], nsin.unsqueeze(1).broadcast_to([P, nh, h]), ALU.mult)
                dve.tensor_tensor(bv[:, :, 1, :], sv[:, :, 0, :], sin.unsqueeze(1).broadcast_to([P, nh, h]),
                                  ALU.mult).then_inc(s["rope_mul"], 1)

            dve.memset(kps[:, :, :], 0.0)
            dve.memset(kpd[:, :, :], 0.0)
            dve.memset(gl8[:, :, :], NEG)
            dve.memset(key[:, :, :], -1.0)
            dve.memset(comb[:, :, :], 0.0).then_inc(s["cleared"], 1)
            dve.wait_ge(s["params_landed"], 16 * N_FIRST)
            dve.wait_ge(s["const_landed"], 16)
            dve.tensor_scalar(nsink[:, :, :], sink[:, :, :], -1.0, None, ALU.mult)
            dve.tensor_tensor(sublg[:, :], subln[:, :], cst[:, O_LAM + L:O_LAM + 2 * L], ALU.mult)
            dve.drain()
            dve.wait_ge(s["x_landed"], 16)
            with dve.Fori(0, L) as l:
                norm_rows(l, 0)
                for n in range(2):
                    q, k = (lqk[:, 2 * n + c, bass.ds(l, 1), :].rearrange("p a n -> p (a n)") for c in range(2))
                    dve.tensor_tensor(msf[:, n * DQK:(n + 1) * DQK], q, k, ALU.mult)
                dve.drain()
                i = dve.tensor_reduce(lam[:, 0:2], msf[:, 0:2 * DQK].rearrange("p (n d) -> p n d", n=2), AX, ALU.add)
                i.then_inc(s["lam_sum"], 1)
                dve.wait_ge(s["lam_exp"], l + 1)
                dve.tensor_tensor(neglam[:, :], lam[:, 3:4], lam[:, 2:3], ALU.subtract)
                dve.drain()
                dve.tensor_tensor(neglam[:, :], neglam[:, :], cst[:, bass.ds(l + O_LAM, 1)], ALU.subtract)
                turn_out(l, 0, g_attn)
                for tt in range(TT):
                    dve.wait_ge(s["low_ready"], 4 * l + 3 + tt)
                    rope(l, tt, tt, ps[:, 2 + tt, MLA_KVR:MLA_KVR + ROPE], 1, 32)
                for tt in range(TT):
                    dve.wait_ge(s["u_ps"], 10 * l + 5 + tt)
                    rope(l, 2 + tt, tt, ps[:, 4 + tt, :], 8, 64)
                for b in range(3):
                    nch = 2 if b < 2 else 1
                    dve.wait_ge(s["lowT_ps"], 3 * l + b + 1)
                    g = lay(g_low, l)
                    dve.tensor_tensor(lowT[:, 2 * b:2 * b + nch, :], ps[:, 2 + b, 0:nch * T].rearrange("p (c t) -> p c t", c=nch),
                                      g[:, 2 * b:2 * b + nch].unsqueeze(2).broadcast_to([P, nch, T]), ALU.mult).then_inc(s["lowT_sb"], 1)
                for tt in range(TT):
                    dve.wait_ge(s["v_sb"], 4 * l + 1 + tt)
                    rope(l, 4 + tt, tt, ps[:, 6 + tt, 128:384], 8, 32)
                for tt in range(TT):
                    dve.wait_ge(s["v_sb"], 4 * l + 3 + tt)
                    rope(l, 6 + tt, tt, ps[:, tt, 0:256], 8, 32)
                for j, (bank, tt, half) in enumerate(UQ_JOBS):
                    dve.wait_ge(s["q_nope"], 4 * l + j + 1)
                    rope(l, 8 + j, tt, ps[:, bank, 0:288].rearrange("p (h d) -> p h d", h=3)[:, :, NOPE:MLA_QK], 3, 32)
                for j in (1, 3, 5, 7, 9):
                    dve.wait_ge(s["T_ps"], 10 * l + j + 1)
                    v = ps[:, T_BANKS[j], :].rearrange("p (c t) -> p c t", c=2)
                    if j == 1:
                        dve.tensor_scalar(qTs[:, 2, :], v[:, 0, :], HD ** -0.5, None, ALU.mult)
                        dve.tensor_copy(kps[0:64, 0, :], v[0:64, 1, :])
                        i = dve.tensor_copy(kps[64:128, 1, :], v[64:128, 1, :])
                    elif j == 3:
                        for m in range(2 * DIFF_H):
                            r0 = 32 * (m % 4)
                            i = dve.tensor_copy(kpd[r0:r0 + 32, m, :], v[r0:r0 + 32, m // 4, :])
                    elif j < 7:
                        i = dve.tensor_scalar(qTm[0:MLA_QK, 2 * (j - 4):2 * (j - 4) + 2, :], v[0:MLA_QK], MLA_QK ** -0.5,
                                              None, ALU.mult)
                    else:
                        i = dve.tensor_copy(kTm[0:MLA_QK, 2 * (j - 7):2 * (j - 7) + 2, :], v[0:MLA_QK])
                    i.then_inc(s["T_dve"], 1)
                for t_ in range(NMAPS + 5):
                    if t_ < NMAPS:
                        kind, n = MAPS[t_][4:6]
                        v = ps[:, t_ % 3, :].rearrange("p (t k) -> p t k", t=TT)
                        dve.wait_ge(s["score_ps"], NMAPS * l + t_ + 1)
                        if kind == "swa":
                            dve.wait_ge(s["prob_ready"], NMAPS * l + t_)
                            past(dve)
                            for qt in range(TT):
                                dve.tensor_tensor_reduce(ms[:, qt, :], v[:, qt, :], mask[:, qt, :], 1.0, NEG, ALU.add, ALU.max,
                                                         rmax[:, t_, qt:qt + 1])
                            dve.drain()
                            ns = nsink[:, bass.ds(l, 1), n:n + 1].rearrange("p a n -> p (a n)")
                            i = dve.tensor_scalar(nmax[:, t_, :], rmax[:, t_, :], -1.0, ns, ALU.mult, ALU.min)
                        else:
                            i = dve.tensor_reduce(nmax[:, t_, :], v, AX, ALU.max, negate=True)
                        i.then_inc(s["nmax_ready"], 1)
                    m = unit_at(t_ - 3)
                    if m is not None and m % 2 == 1:
                        dve.wait_ge(s["probT_ps"], NUNITS * l + m + 1)
                        if m >= 4:
                            dve.wait_ge(s["o_ps"], len(GROUPS) * l + group_of(m - 4) + 1)
                        dve.tensor_copy(probT[m % 4], ps[:, 4, :].rearrange("p (k t) -> p k t", k=TT)).then_inc(s[TURNED[1]], 1)
                    m = t_ - 1
                    if 0 <= m < NMAPS:
                        kind, n = MAPS[m][4:6]
                        dve.wait_ge(s["prob_ready"], NMAPS * l + m + 1)
                        if kind == "swa":
                            dve.tensor_tensor(psum_[:, m, :], psum_[:, m, :], esink[:, n, :], ALU.add)
                            dve.drain()
                        i = dve.reciprocal(rinv[:, m, :], psum_[:, m, :])
                        dve.drain()
                        if m < NPLAIN:
                            for qt in range(TT):
                                i = dve.tensor_scalar(prob[m % 4][:, qt, :], prob[m % 4][:, qt, :], rinv[:, m, qt:qt + 1],
                                                      None, ALU.mult)
                            i.then_inc(s["scaled"], 1)
                        elif n % 2 == 1:
                            dve.tensor_scalar(rinv[:, m, :], rinv[:, m, :], neglam[:, 0:1], None, ALU.mult)
                            p0, p1 = prob[(m - 1) % 4], prob[m % 4]
                            for qt in range(TT):
                                dve.tensor_scalar(p0[:, qt, :], p0[:, qt, :], rinv[:, m - 1, qt:qt + 1], None, ALU.mult)
                            dve.drain()
                            for qt in range(TT):
                                i = dve.scalar_tensor_tensor(out=p0[:, qt, :], in0=p1[:, qt, :], scalar=rinv[:, m, qt:qt + 1],
                                                             in1=p0[:, qt, :], op0=ALU.mult, op1=ALU.add)
                            i.then_inc(s["scaled"], 1)
                    g_ = group_at(t_ - 4)
                    if g_ is not None:
                        units = GROUPS[g_]
                        dve.wait_ge(s["o_ps"], len(GROUPS) * l + g_ + 1)
                        if len(units) == 2:
                            i = dve.tensor_copy(hT[:, units[0] // 2, :], ps[:, 5 + g_ % 2, 0:T])
                        else:
                            h = units[0] - NPLAIN
                            i = dve.tensor_copy(odiff[:, :, h * DV:(h + 1) * DV],
                                                ps[:, 5 + g_ % 2, 0:TT * DV].rearrange("p (t d) -> p t d", t=TT))
                        i.then_inc(s["o_sb"], 1)
                dve.drain()
                od = odiff
                dve.tensor_tensor(ms[:, :, :], od, od, ALU.mult)
                dve.drain()
                dve.tensor_reduce(dssq[:, :], msf.rearrange("p (h d) -> p h d", d=DV), AX, ALU.add).then_inc(s["dsq_ready"], 1)
                dve.wait_ge(s["drms_ready"], l + 1)
                for tt in range(TT):
                    v = od[:, tt, :].rearrange("p (h d) -> p h d", d=DV)
                    i = dve.tensor_tensor(v, v, drs[:, 4 * tt:4 * tt + 4].unsqueeze(2).broadcast_to([P, 4, DV]), ALU.mult)
                i.then_inc(s["dnorm_ready"], 1)
                dve.wait_ge(s["oT_ps"], l + 1)
                dve.tensor_scalar(hT[:, 6:8, :], ps[:, 0, :].rearrange("p (c t) -> p c t", c=2), col(sublg, l), None,
                                  ALU.mult).then_inc(s["oT_dve"], 1)
                for j in range(4):
                    tt, half = j // 2, j % 2
                    dve.wait_ge(s["wout_ps"], 4 * l + j + 1)
                    v = x[:, tt, half * 512:(half + 1) * 512]
                    dve.tensor_tensor(v, v, ps[:, 4 + j, :], ALU.add).then_inc(s["x_mixed"], 1)
                dve.drain()
                norm_rows(l, 1)
                dve.wait_ge(s["router_landed"], 16 * N_SECOND)
                dve.tensor_copy(w_rl[:, :, :], w_r[:, bass.ds(l, 1), :, :].rearrange("p a k n -> p (a k) n"))
                turn_out(l, 1, g_ffn)
                dve.wait_ge(s["logitT_ps"], l + 1)
                dve.tensor_copy(logitT, ps[0:G + NE, 4, 0:T]).then_inc(s["logitT_sb"], 1)
                dve.wait_ge(s["logit_ps"], l + 1)
                lg = ps[:, 4, 0:128].rearrange("p (t n) -> p t n", t=TT)
                bias = lay(rbias, l).unsqueeze(1)
                dve.tensor_tensor(gl8[:, :, 0:G], lg[:, :, 0:G], bias[:, :, 0:G].broadcast_to([P, TT, G]), ALU.add)
                dve.tensor_tensor(el[:, :, :], lg[:, :, G:G + NE], bias[:, :, G:G + NE].broadcast_to([P, TT, NE]), ALU.add)
                dve.drain()
                for tt in range(TT):
                    dve.max(gtop[:, tt, :], gl8[:, tt, :])
                dve.drain()
                dve.tensor_scalar(ngm[:, :].unsqueeze(2), gtop[:, :, 0:1], -1.0, None, ALU.mult).then_inc(s["rt_dve"], 1)
                for tt in range(TT):
                    dve.max_index(gidx[:, tt, :], gtop[:, tt, :], gl8[:, tt, :])
                dve.drain()
                dve.tensor_copy(fidx[:, 0, :, :], gidx[:, :, :])
                dve.drain()
                dve.tensor_tensor(ohg[:, :, :], iota[:, 0:G].unsqueeze(1).broadcast_to([P, TT, G]),
                                  fidx[:, 0, :, 0:1].broadcast_to([P, TT, G]), ALU.is_equal)
                dve.drain()
                dve.tensor_tensor(prod[:, :, :, :], el[:, :, :].rearrange("p t (g e) -> p t g e", g=G),
                                  ohg[:, :, :].unsqueeze(3).broadcast_to([P, TT, G, E]), ALU.mult)
                dve.drain()
                dve.tensor_reduce(esel[:, :, :], prod[:, :, :, :].rearrange("p t g e -> p t e g"), AX, ALU.add)
                dve.drain()
                for tt in range(TT):
                    dve.max(etop[:, tt, :], esel[:, tt, :])
                dve.drain()
                dve.tensor_tensor(wts[:, 0, :].unsqueeze(2), etop[:, :, 1:2], etop[:, :, 0:1], ALU.subtract).then_inc(s["rt_dve"], 1)
                for tt in range(TT):
                    dve.max_index(eidx[:, tt, :], etop[:, tt, :], esel[:, tt, :])
                dve.drain()
                dve.tensor_copy(fidx[:, 1, :, :], eidx[:, :, :])
                dve.drain()
                io8 = iota[:, 0:E].unsqueeze(1).broadcast_to([P, TT, E])
                for c in range(2):
                    dve.tensor_tensor(oh[:, c, :, :], io8, fidx[:, 1, :, c:c + 1].broadcast_to([P, TT, E]), ALU.is_equal)
                dve.drain()
                dve.tensor_tensor(oh[:, 2, :, :], oh[:, 0, :, :], oh[:, 1, :, :], ALU.add)
                dve.drain()
                dve.tensor_reduce(pmax[:, :, :], oh[:, 2, :, :].rearrange("p t (q w) -> p t q w", w=2), AX, ALU.max)
                dve.drain()
                dve.tensor_tensor(member[:, :, :].rearrange("p t (g q) -> p t g q", g=G),
                                  pmax[:, :, :].unsqueeze(2).broadcast_to([P, TT, G, 4]),
                                  ohg[:, :, :].unsqueeze(3).broadcast_to([P, TT, G, 4]), ALU.mult).then_inc(s["member_ready"], 1)
                dve.wait_ge(s["rt_exp"], 2 * l + 2)
                dve.tensor_scalar(wts[:, 2, :], wts[:, 1, :], 1.0, None, ALU.add)
                dve.drain()
                dve.tensor_tensor(wts[:, 2, :], wts[:, 2, :], gsum[:, :], ALU.mult)
                dve.drain()
                dve.reciprocal(wts[:, 3, :], wts[:, 2, :])
                dve.drain()
                dve.tensor_tensor(wts[:, 4, :], wts[:, 3, :], wts[:, 1, :], ALU.mult)
                dve.drain()
                for c in range(2):
                    dve.tensor_tensor(oh[:, 3 + c, :, :], oh[:, c, :, :], wts[:, 3 + c, :].unsqueeze(2).broadcast_to([P, TT, E]), ALU.mult)
                dve.drain()
                dve.tensor_tensor(oh[:, 3, :, :], oh[:, 3, :, :], oh[:, 4, :, :], ALU.add)
                dve.drain()
                for tt in range(TT):
                    dve.tensor_tensor(comb[:, tt, 0:NE].rearrange("p (g e) -> p g e", g=G),
                                      oh[:, 3, tt, :].unsqueeze(1).broadcast_to([P, G, E]),
                                      ohg[:, tt, :].unsqueeze(2).broadcast_to([P, G, E]), ALU.mult)
                dve.wait_ge(s["rank_ps"], l + 1)
                for tt in range(TT):
                    dve.scalar_tensor_tensor(out=key[:, tt, 0:NPAIR], in0=ps[:, 5, 32 * tt:32 * tt + NPAIR], scalar=1.0,
                                             in1=member[:, tt, :], op0=ALU.add, op1=ALU.mult)
                dve.tensor_reduce(cnt[:, 0:1], ps[:, 5, 64:64 + NPAIR], AX, ALU.max)
                dve.drain()
                dve.tensor_scalar(key[:, :, 0:NPAIR], key[:, :, 0:NPAIR], 1.0, None, ALU.subtract)
                dve.tensor_scalar(cnt[:, 1:2], cnt[:, 0:1], float(SLOTS), None, ALU.is_gt)
                dve.tensor_scalar(cnt[:, 2:3], cnt[:, 0:1], float(2 * SLOTS), None, ALU.is_gt)
                dve.tensor_scalar(cnt[:, 3:4], cnt[:, 0:1], float(3 * SLOTS), None, ALU.is_gt)
                dve.drain()
                dve.tensor_reduce(cnt[:, 0:1], cnt[:, 1:4], AX, ALU.add)
                dve.drain()
                dve.tensor_scalar(npass_t[:, :], cnt[:, 0:1], 1.0, None, ALU.add).then_inc(s["routed"], 1)
                npass = load_npass(dve, l)

                def build_pick(pair):
                    kv = key[:, :, bass.ds(pair, 2)].unsqueeze(3).broadcast_to([P, TT, 2, SLOTS])
                    for tt in range(TT):
                        i = dve.tensor_tensor(pick[:, tt, :].rearrange("p (q s) -> p q s", q=2),
                                              iota.unsqueeze(1).broadcast_to([P, 2, SLOTS]), kv[:, tt], ALU.is_equal)
                    i.then_inc(s["pick_ready"], 1)

                def gather_out(l, q):
                    dve.wait_ge(s["comb_ps"], q + 1)
                    dve.tensor_copy(cc[0:64, :], ps[0:64, 6, 0:2])
                    dve.tensor_copy(cc[64:128, :], ps[64:128, 6, 2:4]).then_inc(s["comb_sb"], 1)
                    g = lay(g_ffn, l)
                    for c, (bank, k0) in enumerate(((5, 0), (4, 4))):
                        dve.wait_ge(s["gath_ps"], 2 * q + c + 1)
                        dve.tensor_tensor(hTg[:, k0:k0 + 4, :], ps[:, bank, :].rearrange("p (k s) -> p k s", k=4),
                                          g[:, k0:k0 + 4].unsqueeze(2).broadcast_to([P, 4, P]), ALU.mult).then_inc(s["gath_sb"], 1)

                with dve.Fori(0, npass):
                    done = dve.snap(passes)
                    dve.drain()
                    build_pick(0)
                    gather_out(l, done * (NIT + 1))
                    with dve.Fori(0, NIT) as i:
                        u = done * NIT + i
                        q = done * (NIT + 1) + i
                        dve.wait_ge(s["pickT_ps"], u + 1)
                        build_pick(2 * i + 2)
                        dve.drain()
                        dve.wait_ge(s["silu_a"], u + 1)
                        dve.scalar_tensor_tensor(out=hid[0], in0=sil[0], scalar=cc[:, 0:1], in1=ps[:, 6, F:2 * F],
                                                 op0=ALU.mult, op1=ALU.mult).then_inc(s["hid_a"], 1)
                        dve.wait_ge(s["silu_b"], u + 1)
                        dve.scalar_tensor_tensor(out=hid[1], in0=sil[1], scalar=cc[:, 1:2], in1=ps[:, 7, F:2 * F],
                                                 op0=ALU.mult, op1=ALU.mult).then_inc(s["hid_b"], 1)
                        dve.drain()
                        gather_out(l, q + 1)
                        dve.wait_ge(s["hidT_ps"], 2 * u + 2)
                        dve.tensor_copy(hidT[1], ps[:, 7, 0:T].rearrange("p (j s) -> p j s", j=2)).then_inc(s["hidTb_sb"], 1)
                        dve.wait_ge(s["y_ps"], u + 1)
                        dve.tensor_copy(y_sb[:, 0, :], ps[:, 4, :]).then_inc(s["y_dve"], 1)
                    dve.drain()
                    dve.tensor_scalar(key[:, :, 0:NPAIR], key[:, :, 0:NPAIR], float(SLOTS), None, ALU.subtract)
                    dve.reg_add(passes, passes, 1)
                dve.wait_ge(s["acc_ready"], dve.snap(passes) * NIT)
                dve.tensor_copy(x[:, 1, :].rearrange("p (b n) -> p b n", b=2), ps[:, 2:4, :]).then_inc(s["x_dve"], 1)
                dve.drain()
            dve.tensor_tensor_reduce(hAf[:, D:2 * D], x[:, 1, :], x[:, 1, :], 1.0, 0.0, ALU.mult, ALU.add,
                                     ssq[:, 1:2]).then_inc(s["sq_dve"], 1)
            dve.wait_ge(s["rms_ready"], 2 * L + 1)
            dve.wait_ge(s["x_act"], L)
            for tt in range(TT):
                dve.scalar_tensor_tensor(out=hT[:, 4 * tt:4 * tt + 4, :].rearrange("p k n -> p (k n)"), in0=x[:, tt, :],
                                         scalar=rs[:, tt:tt + 1], in1=g_fin[:, :], op0=ALU.mult,
                                         op1=ALU.mult).then_inc(s["out_ready"], 1)


N_FIRST, N_SECOND = 8 + 2 * L, 4 + 2 * L

_INS = ['x', 'attn_norm', 'w_in', 'mla_q_norm', 'mla_kv_norm', 'mla_w_uq', 'mla_w_ukv', 'swa_sink', 'diff_lq1', 'diff_lk1',
        'diff_lq2', 'diff_lk2', 'diff_subln', 'w_out', 'ffn_norm', 'router_group', 'router_group_bias', 'router_expert',
        'router_expert_bias', 'w_gate', 'w_up', 'w_down', 'final_norm']


def kernel(**inputs):
    import concourse.bacc as _bacc
    from concourse.bass_utils import run_bass_kernel_spmd as _run

    nc = _bacc.Bacc("TRN2", target_bir_lowering=False, num_devices=1)
    arrays = {"const_dram": constants()}
    for name in _INS:
        arrays[f"in_{name}_dram"] = np.ascontiguousarray(inputs[name])
    args = [nc.dram_tensor(n, a.shape, mybir.dt.from_np(a.dtype), kind="ExternalInput").ap() for n, a in arrays.items()]
    args.append(nc.dram_tensor("out_0_dram", (1, T, D), F32, kind="ExternalOutput").ap())
    encoder_kernel(nc, *args)
    r = _run(nc, [arrays], core_ids=[0])
    return r.results[0]["out_0_dram"]
```

```python
import math

import concourse.bass as bass
import concourse.mybir as mybir
import numpy as np
from concourse.alu_op_type import AluOpType as ALU

F32 = mybir.dt.float32
I32 = mybir.dt.int32
U32 = mybir.dt.uint32
ACT = mybir.ActivationFunctionType
AX = mybir.AxisListType.X

P = 128
D = 1024
T = 256
TT = T // P
L = 2
KD = D // P
EPS = 1e-6

MLA_H, MLA_QR, MLA_KVR, NOPE, ROPE, MLA_V = 6, 384, 256, 64, 32, 64
MLA_QK = NOPE + ROPE
SWA_H, SWA_KV, HD, WINDOW = 6, 2, 64, 128
DIFF_H, DQK, DV = 4, 32, 64
IN_W = MLA_QR + MLA_KVR + ROPE + SWA_H * HD + 2 * SWA_KV * HD + 4 * DIFF_H * DQK + DIFF_H * DV
NMAPS = MLA_H + SWA_H + 2 * DIFF_H

G, E, F = 4, 8, 256
NE = G * E
NPAIR = NE // 2
SLOTS = 64
NIT = NPAIR // 2
NEG = -3.0e38

C_Q, C_KV, C_SQK, C_VDQ, C_DKV = (0, 384), (384, 288), (672, 512), (1184, 384), (1568, 512)
assert C_DKV[0] + C_DKV[1] == IN_W

O_ID, O_TRI, O_ONE, O_IOTA = 0, P, 2 * P, 3 * P
O_C64 = O_IOTA + SLOTS
O_C32 = O_C64 + 3 * TT * 32
O_MASK = O_C32 + 3 * TT * 16
O_LAM = O_MASK + TT * T
N_CONST = O_LAM + 2 * L


def constants():
    c = np.zeros((P, N_CONST), np.float32)
    c[:, O_ID:O_ID + P] = np.eye(P)
    c[:, O_TRI:O_TRI + P] = np.triu(np.ones((P, P)), 1)
    c[:, O_ONE:O_ONE + P] = 1.0
    c[:, O_IOTA:O_IOTA + SLOTS] = np.arange(SLOTS)
    for off, dim in ((O_C64, 64), (O_C32, 32)):
        inv = (np.float32(1.0) / (np.float32(10000.0) ** (np.arange(0, dim, 2, dtype=np.float32) / np.float32(dim))))
        ang = np.arange(T, dtype=np.float32)[:, None] * inv[None, :].astype(np.float32)
        h = dim // 2
        for n, t in enumerate((np.cos(ang), np.sin(ang), -np.sin(ang))):
            for tt in range(TT):
                c[:, off + (n * TT + tt) * h:off + (n * TT + tt + 1) * h] = t[tt * P:(tt + 1) * P]
    q = np.arange(T).reshape(TT, P).T[:, :, None]
    c[:, O_MASK:O_MASK + TT * T] = np.where(np.abs(q - np.arange(T)[None, None]) <= WINDOW, 0.0, -1e30).reshape(P, TT * T)
    for l in range(L):
        init = 0.8 - 0.6 * math.exp(-0.3 * l)
        c[:, O_LAM + l] = init
        c[:, O_LAM + L + l] = 1.0 - init
    return c


def encoder_kernel(nc, const, x_in, attn_norm, w_in, mla_q_norm, mla_kv_norm, w_uq, w_ukv, swa_sink, lq1, lk1, lq2, lk2,
                   diff_subln, w_out, ffn_norm, router_group, router_group_bias, router_expert, router_expert_bias,
                   w_gate, w_up, w_down, final_norm, out):
    def sb(name, shape, dt=F32):
        return nc.alloc_sbuf_tensor(name, shape, dt)

    ps = nc.alloc_psum_tensor("banks", [P, 8, 512], F32)

    ring = sb("ring", [P, 14, IN_W])
    cst = sb("cst", [P, N_CONST])
    g_attn = sb("g_attn", [P, L, KD])
    g_ffn = sb("g_ffn", [P, L, KD])
    g_low = sb("g_low", [P, L, 5])
    sink = sb("sink", [P, L, SWA_H])
    nsink = sb("nsink", [P, L, SWA_H])
    lqk = sb("lqk", [P, 4, L, DQK])
    subln = sb("subln", [P, L])
    sublg = sb("sublg", [P, L])
    rbias = sb("rbias", [P, G + NE])
    w_r = sb("w_r", [P, KD, G + NE])
    g_fin = sb("g_fin", [P, D])

    x = sb("x", [P, TT, D])
    hA = sb("hA", [P, TT, KD, P])
    hAf = hA[:, :, :, :].rearrange("p t k j -> p (t k j)")
    hT = sb("hT", [P, KD, T])
    shared = sb("shared", [P, 4992])
    qTm = shared[:, 0:1536].rearrange("p (h t) -> p h t", h=MLA_H)
    kTm = shared[:, 1536:3072].rearrange("p (h t) -> p h t", h=MLA_H)
    lowT = shared[:, 1536:2816].rearrange("p (c t) -> p c t", c=5)
    km = shared[:, 3072:4224].rearrange("p (t h d) -> p t h d", t=TT, h=MLA_H)
    vm = shared[:, 4224:4992].rearrange("p (t d) -> p t d", t=TT)
    hTg = shared[:, 0:1024].rearrange("p (k s) -> p k s", k=KD)
    pick = shared[:, 1024:1280].rearrange("p (t s) -> p t s", t=TT)
    pickT = shared[:, 1280:1536]
    sil = [shared[:, 1536:1792], shared[:, 1792:2048]]
    hid = [shared[:, 2048:2304], shared[:, 2304:2560]]
    hidT = [shared[:, 2560 + 256 * n:2816 + 256 * n].rearrange("p (j s) -> p j s", j=2) for n in range(2)]
    y_sb = shared[:, 3072:4096].rearrange("p (b n) -> p b n", b=2)
    low = sb("low", [P, TT, MLA_QR + MLA_KVR])
    qm = low[:, :, 0:MLA_H * MLA_QK].rearrange("p t (h d) -> p t h d", h=MLA_H)
    rq = sb("rq", [P, TT, D])
    vsd = sb("vsd", [P, TT, SWA_KV * HD + DIFF_H * DV])
    kro = sb("kro", [P, TT, ROPE])
    qTs = sb("qTs", [P, 3, T])
    kps = sb("kps", [P, SWA_KV, T])
    qTd = sb("qTd", [P, 2, T])
    kpd = sb("kpd", [P, 2 * DIFF_H, T])
    ms = sb("ms", [P, TT, T])
    msf = ms[:, :, :].rearrange("p t n -> p (t n)")
    masked = [ms[:, :, :], low[:, :, 256:512]]
    logitT = msf[0:G + NE, 0:T]
    tmpA = [hAf[:, 0:512], hAf[:, 1024:1536]]
    tmpB = [hAf[:, 512:1024], hAf[:, 1536:2048]]
    hTf = hT[:, :, :].rearrange("p k t -> p (k t)")

    def rope_tmps(r):
        if r < 10:
            return tmpA[r % 2], tmpB[r % 2]
        room = msf if r == 10 else hTf[:, 1536:2048]
        return room[:, 0:256], room[:, 256:512]

    prob = [hAf[:, 512 * n:512 * n + 512].rearrange("p (t k) -> p t k", t=TT) for n in range(4)]
    rqf = rq[:, :, :].rearrange("p t n -> p (t n)")
    probT = [rqf[:, 512 * n:512 * n + 512].rearrange("p (k t) -> p k t", k=TT) for n in range(4)]
    odiff = low[:, :, 0:DIFF_H * DV]
    nhalf = sb("nhalf", [P, 8])
    ssq = sb("ssq", [P, TT])
    rs = sb("rs", [P, TT])
    ssc = sb("ssc", [P, 4])
    rsc = sb("rsc", [P, 4])
    dssq = sb("dssq", [P, 8])
    drs = sb("drs", [P, 8])
    lam = sb("lam", [P, 4])
    neglam = sb("neglam", [P, 1])
    nmax = sb("nmax", [P, NMAPS, TT])
    rmax = sb("rmax", [P, NMAPS, TT])
    psum_ = sb("psum_", [P, NMAPS, TT])
    esink = sb("esink", [P, SWA_H, TT])
    rinv = sb("rinv", [P, NMAPS, TT])
    gl8 = sb("gl8", [P, TT, 8])
    el = sb("el", [P, TT, NE])
    prod = sb("prod", [P, TT, G, E])
    gtop = sb("gtop", [P, TT, 8])
    gidx = sb("gidx", [P, TT, 8], U32)
    etop = sb("etop", [P, TT, 8])
    eidx = sb("eidx", [P, TT, 8], U32)
    fidx = sb("fidx", [P, 2, TT, 8])
    esel = sb("esel", [P, TT, E])
    ngm = sb("ngm", [P, TT])
    gsum = sb("gsum", [P, TT])
    gexp = sb("gexp", [P, TT, G])
    wts = sb("wts", [P, 5, TT])
    ohg = sb("ohg", [P, TT, G])
    oh = sb("oh", [P, 5, TT, E])
    pmax = sb("pmax", [P, TT, 4])
    member = sb("member", [P, TT, NPAIR])
    key = sb("key", [P, TT, NPAIR + 2])
    comb = sb("comb", [P, TT, NE + 4])
    cc = sb("cc", [P, 2])
    cnt = sb("cnt", [P, 4])
    npass_t = sb("npass_t", [P, 1], I32)

    ident = cst[:, O_ID:O_ID + P]
    tri = cst[:, O_TRI:O_TRI + P]
    ones = cst[:, O_ONE:O_ONE + P]
    iota = cst[:, O_IOTA:O_IOTA + SLOTS]
    mask = cst[:, O_MASK:O_MASK + TT * T].rearrange("p (t k) -> p t k", t=TT)

    def table(dim, which, tt):
        off, h = (O_C64, 32) if dim == 64 else (O_C32, 16)
        return cst[:, off + (which * TT + tt) * h:off + (which * TT + tt + 1) * h]

    s = {n: nc.alloc_semaphore(n) for n in (
        "params_landed", "router_landed", "const_landed", "x_landed", "cleared", "sublg_ready",
        "landed_a", "landed_b", "landed_da", "landed_db", "landed_uq", "landed_ukv", "landed_wo",
        "freed_a", "freed_b", "freed_da", "freed_db", "freed_up",
        "sq_act", "sq_dve", "rms0_ready", "rms1_ready", "h_act", "h_dve", "passed", "hT_ps", "hT_sb",
        "u_ps", "low_sq", "low_rms", "low_ready", "v_sb", "rope_mul", "rope_add", "lowT_ps", "lowT_sb",
        "up_ps", "q_nope", "kv_sb", "krope_sb", "T_ps", "T_act", "T_dve", "lam_sum", "lam_exp",
        "score_ps", "nmax_ready", "prob_ready", "probT_ps", "probT_act", "probT_dve", "o_ps", "o_act", "o_dve",
        "dsq_ready", "drms_ready", "dnorm_ready", "oT_ps", "oT_dve", "scaled", "wout_ps", "x_mixed",
        "logit_ps", "logitT_ps", "logitT_sb", "rt_dve", "rt_exp", "member_ready", "rank_ps", "routed", "acc_ready",
        "pick_ready", "pickT_ps", "pickT_sb", "comb_ps", "comb_sb", "gath_ps", "gath_sb",
        "guA_ps", "guB_ps", "silu_a", "silu_b", "hid_a", "hid_b", "hidT_ps", "hidTa_sb", "hidTb_sb",
        "y_ps", "y_act", "y_dve", "x_act", "x_dve", "out_ready", "out_landed")}

    gate_d = w_gate.rearrange("l g e (p k) f -> (l g e) p (k f)", k=KD)
    up_d = w_up.rearrange("l g e (p k) f -> (l g e) p (k f)", k=KD)
    down_d = w_down.rearrange("l g e (j p) n -> (l g e) p j n", p=P)
    win_d = w_in.rearrange("l (p k) n -> l p k n", k=KD)
    wout_d = w_out.rearrange("l (m j p) n -> l m p j n", j=2, p=P)
    wuq_d = w_uq.rearrange("l (c p) n -> l p c n", p=P)
    wukv_d = w_ukv.rearrange("l (c p) n -> l p c n", p=P)
    x_d = x_in.rearrange("b (t p) d -> p (b t) d", p=P)
    out_d = out.rearrange("b (t p) d -> p (b t) d", p=P)

    def dyn(ap, i):
        return ap[bass.ds(i, 1)].rearrange("a p n -> (a p) n") if len(ap.shape) == 3 else \
            ap[bass.ds(i, 1)].rearrange("a p j n -> (a p) j n")

    def wslot(n, j=2):
        return ring[:, n, 0:2048].rearrange("p (j n) -> p j n", j=j)

    def col(tensor, l):
        return tensor[:, bass.ds(l, 1)]

    def lay(tensor, l):
        return tensor[:, bass.ds(l, 1), :].rearrange("p a n -> p (a n)")

    def past(eng):
        eng.sem_inc(s["passed"], 1)

    def load_npass(eng, l):
        eng.wait_ge(s["routed"], l + 1)
        past(eng)
        return eng.value_load(npass_t[0:1, 0:1], min_val=1, max_val=T // SLOTS)

    WOUT_SLOT = (12, 13, 8, 9)
    WOUT_BANKS = (7, 4, 5, 6)

    def wout_part(l, m):
        return wout_d[bass.ds(l, 1), m].rearrange("a p j n -> (a p) j n")

    IN_JOBS = [(0, 0, C_Q), (1, 1, C_Q), (2, 0, C_KV), (3, 1, C_KV), (4, 0, C_SQK), (5, 1, C_SQK),
               (7, 0, C_VDQ), (2, 1, C_VDQ), (3, 0, C_DKV), (4, 1, C_DKV)]
    UQ_JOBS = [(3, 0, 0), (4, 0, 1), (5, 1, 0), (6, 1, 1)]
    UKV_JOBS = [(0, 0, 0), (1, 0, 1), (7, 1, 0), (2, 1, 1)]
    LOWT_BANKS = (0, 1, 6)
    T_JOBS = [("sq", 5), ("sqk", 6), ("q0", 0), ("q1", 1), ("q2", 7), ("k0", 2), ("k1", 5), ("k2", 6), ("dq", 7), ("dk", 7)]

    def take_turned(eng, pos):
        what, bank = T_JOBS[pos]
        v = ps[:, bank, :].rearrange("p (c t) -> p c t", c=2)

        def scaled(dst, src, f):
            if f == 1.0:
                return eng.copy(dst, src) if eng is nc.scalar else eng.tensor_copy(dst, src)
            return eng.activation(dst, src, ACT.Copy, scale=f) if eng is nc.scalar else \
                eng.tensor_scalar(dst, src, f, None, ALU.mult)

        if what == "sq":
            return scaled(qTs[:, 0:2, :], v, HD ** -0.5)
        if what == "sqk":
            scaled(qTs[:, 2, :], v[:, 0, :], HD ** -0.5)
            scaled(kps[0:64, 0, :], v[0:64, 1, :], 1.0)
            return scaled(kps[64:128, 1, :], v[64:128, 1, :], 1.0)
        if what == "dq":
            return scaled(qTd[:, :, :], v, DQK ** -0.5)
        if what == "dk":
            for m in range(2 * DIFF_H):
                r0 = 32 * (m % 4)
                i = scaled(kpd[r0:r0 + 32, m, :], v[r0:r0 + 32, m // 4, :], 1.0)
            return i
        h0 = 2 * int(what[1])
        return scaled((qTm if what[0] == "q" else kTm)[0:MLA_QK, h0:h0 + 2, :], v[0:MLA_QK],
                      MLA_QK ** -0.5 if what[0] == "q" else 1.0)

    def load_up(eng, l):
        eng.dma_start(ring[:, 12, 0:3 * 576].rearrange("p (c n) -> p c n", c=3), dyn(wuq_d, l)).then_inc(s["landed_uq"], 16)
        eng.dma_start(ring[:, 13, 0:2 * 768].rearrange("p (c n) -> p c n", c=2), dyn(wukv_d, l)).then_inc(s["landed_ukv"], 16)

    def maps():
        for h in range(MLA_H):
            yield (lambda qt, h=h: qTm[0:MLA_QK, h, qt * P:(qt + 1) * P], kTm[0:MLA_QK, h, :],
                   lambda kt, h=h: vm[:, kt, h * MLA_V:(h + 1) * MLA_V], h * MLA_V, "mla", h)
        for h in range(SWA_H):
            c, b = h % 3, h // 3
            yield (lambda qt, c=c: qTs[:, c, qt * P:(qt + 1) * P], kps[:, b, :],
                   lambda kt, b=b: vsd[:, kt, b * HD:(b + 1) * HD], MLA_H * MLA_V + h * HD, "swa", h)
        for m in range(2 * DIFF_H):
            h = m // 2
            yield (lambda qt, m=m: qTd[:, m // 4, qt * P:(qt + 1) * P], kpd[:, m, :],
                   lambda kt, h=h: vsd[:, kt, SWA_KV * HD + h * DV:SWA_KV * HD + (h + 1) * DV],
                   (MLA_H + SWA_H) * HD + h * DV, "diff", m)

    MAPS = list(maps())
    NPLAIN = MLA_H + SWA_H
    NUNITS = NPLAIN + DIFF_H
    GROUPS = [(n, n + 1) for n in range(0, NPLAIN, 2)] + [(n,) for n in range(NPLAIN, NUNITS)]
    def turned(l, n):
        if by_dve(n):
            return s["probT_dve"], (MLA_H // 2) * l + sum(by_dve(i) for i in range(n + 1))
        return s["probT_act"], (NUNITS - MLA_H // 2) * l + sum(not by_dve(i) for i in range(n + 1))

    def group_out(l, g):
        pairs = NPLAIN // 2
        return (s["o_act"], pairs * l + g + 1) if g < pairs else (s["o_dve"], DIFF_H * l + g - pairs + 1)

    def by_dve(n):
        return n < MLA_H and n % 2 == 1

    def unit_of(m):
        return m if m < NPLAIN else NPLAIN + (m - NPLAIN) // 2

    def last_map(n):
        return n if n < NPLAIN else NPLAIN + 2 * (n - NPLAIN) + 1

    def unit_buf(n):
        return (n if n < NPLAIN else last_map(n) - 1) % 4

    def unit_at(m):
        return next((n for n in range(NUNITS) if last_map(n) == m), None)

    def group_of(n):
        return next(g for g, units in enumerate(GROUPS) if n in units)

    def group_at(m):
        return next((g for g, units in enumerate(GROUPS) if last_map(units[-1]) == m), None)

    with nc.Block() as block:

        @block.sync
        def _(sp):
            passes = sp.alloc_register("sp_passes")
            sp.reg_mov(passes, 0)
            sp.dma_start(x[:, :, :], x_d).then_inc(s["x_landed"], 16)
            sp.wait_ge(s["const_landed"], 16)
            def pass_loads(l, p_before):
                with sp.Fori(0, NIT) as i:
                    n = l + 1 + p_before * NIT + i
                    e = l * NE + 4 * i
                    sp.wait_ge(s["freed_a"], n + 1)
                    for m, ex in ((0, 0), (2, 2)):
                        sp.dma_start(ring[:, m, 0:2048], dyn(gate_d, e + ex)).then_inc(s["landed_a"], 16)
                        sp.dma_start(ring[:, m + 1, 0:2048], dyn(up_d, e + ex)).then_inc(s["landed_a"], 16)
                    sp.wait_ge(s["freed_b"], n + 1)
                    for m, ex in ((4, 1), (6, 3)):
                        sp.dma_start(ring[:, m, 0:2048], dyn(gate_d, e + ex)).then_inc(s["landed_b"], 16)
                        sp.dma_start(ring[:, m + 1, 0:2048], dyn(up_d, e + ex)).then_inc(s["landed_b"], 16)
                    sp.wait_ge(s["freed_da"], n + 1)
                    for m, ex in ((8, 0), (9, 2)):
                        sp.dma_start(wslot(m), dyn(down_d, e + ex)).then_inc(s["landed_da"], 16)
                    sp.wait_ge(s["freed_db"], p_before * NIT + i + 1)
                    for m, ex in ((10, 1), (11, 3)):
                        sp.dma_start(wslot(m), dyn(down_d, e + ex)).then_inc(s["landed_db"], 16)

            with sp.Fori(0, L) as l:
                before = sp.snap(passes)
                n = l + before * NIT
                for name, k0 in (("a", 0), ("b", 4)):
                    sp.wait_ge(s["freed_" + name], n + 1)
                    for k in range(k0, k0 + 4):
                        src = win_d[bass.ds(l, 1), :, k, :].rearrange("a p n -> (a p) n")
                        sp.dma_start(ring[:, k, :], src).then_inc(s["landed_" + name], 16)
                sp.wait_ge(s["freed_da"], n + 1)
                for m in (2, 3):
                    sp.dma_start(wslot(WOUT_SLOT[m]), wout_part(l, m)).then_inc(s["landed_da"], 16)
                sp.wait_ge(s["freed_up"], 2 * l + 2)
                past(sp)
                for m in (0, 1):
                    sp.dma_start(wslot(WOUT_SLOT[m]), wout_part(l, m)).then_inc(s["landed_wo"], 16)
                pass_loads(l, before)
                sp.reg_add(passes, passes, 1)
                npass = load_npass(sp, l)
                with sp.If(npass > 1):
                    with sp.Fori(1, npass):
                        pass_loads(l, sp.snap(passes))
                        sp.reg_add(passes, passes, 1)
            sp.wait_ge(s["out_ready"], 2)
            sp.dma_start(out_d, hT[:, :, :].rearrange("p (t k) n -> p t (k n)", t=TT)).then_inc(s["out_landed"], 16)
            sp.wait_ge(s["out_landed"], 16)

        @block.tensor
        def _(pe):
            passes = pe.alloc_register("pe_passes")
            pe.reg_mov(passes, 0)
            for n in ("freed_a", "freed_b", "freed_da", "freed_db", "freed_up"):
                pe.sem_inc(s[n], 1)

            def turn_h(l, which):
                for tt in range(TT):
                    pe.wait_ge(s["h_act" if tt == 0 else "h_dve"], 2 * l + which + 1)
                    for k in range(KD):
                        if which == 0 and tt == 0 and k == 4:
                            pe.wait_ge(s["sq_dve"], 2 * l + 1)
                        t = pe.transpose(ps[:, k // 2, (k % 2) * T + tt * P:(k % 2) * T + (tt + 1) * P], hA[:, tt, k, :], ident)
                        if which == 1 and tt == 0 and k < 2:
                            t.then_inc(s["freed_da" if k == 0 else "freed_up"], 1)
                        if tt == 1 and k % 2 == 1:
                            t.then_inc(s["hT_ps"], 1)

            def prepare(q, free_b=True):
                pe.wait_ge(s["pick_ready"], q + 1)
                for tt in range(TT):
                    mm = pe.matmul(ps[:, 6, 0:4], pick[:, tt, :], comb[:, tt, bass.ds(q_pair[0], 4)],
                                   start=(tt == 0), stop=(tt == TT - 1))
                    if tt == 0 and free_b:
                        mm.then_inc(s["freed_b"], 1)
                mm.then_inc(s["comb_ps"], 1)
                for bank, k0 in ((5, 0), (4, 4)):
                    for k in range(k0, k0 + 4):
                        for tt in range(TT):
                            mm = pe.matmul(ps[:, bank, (k - k0) * P:(k - k0 + 1) * P], hA[:, tt, k, :], pick[:, tt, :],
                                           start=(tt == 0), stop=(tt == TT - 1))
                    mm.then_inc(s["gath_ps"], 1)

            q_pair = [0]
            with pe.Fori(0, L) as l:
                before = pe.snap(passes)
                n = l + before * NIT
                if True:
                    pe.wait_ge(s["const_landed"], 16)
                    turn_h(l, 0)
                    pe.wait_ge(s["hT_sb"], 8 * l + 4)

                    def project_in(j, k0=0, k1=KD):
                        bank, tt, (c0, w) = IN_JOBS[j]
                        for k in range(k0, k1):
                            mm = pe.matmul(ps[:, bank, 0:w], hT[:, k, tt * P:(tt + 1) * P], ring[:, k, c0:c0 + w],
                                           start=(k == 0), stop=(k == KD - 1))
                            if j == 8 and k == 0:
                                mm.then_inc(s["freed_up"], 1)
                        if k1 == KD:
                            mm.then_inc(s["u_ps"], 1)

                    pe.wait_ge(s["landed_a"], 64 * n + 64)
                    for j in range(6):
                        project_in(j, 0, KD // 2)
                    pe.wait_ge(s["landed_b"], 64 * n + 64)
                    for j in range(6):
                        project_in(j, KD // 2, KD)
                    pe.wait_ge(s["low_ready"], 4 * l + 4)
                    for c in range(5):
                        for tt in range(TT):
                            t = pe.transpose(ps[:, LOWT_BANKS[c // 2], (c % 2) * T + tt * P:(c % 2) * T + (tt + 1) * P],
                                             low[:, tt, c * P:(c + 1) * P], ident)
                        if c in (1, 3, 4):
                            t.then_inc(s["lowT_ps"], 1)
                    project_in(6)
                    pe.wait_ge(s["rope_mul"], 12 * l + 1)
                    project_in(7)
                    pe.wait_ge(s["lowT_sb"], 3 * l + 3)
                    pe.wait_ge(s["landed_uq"], 16 * l + 16)
                    pe.wait_ge(s["landed_ukv"], 16 * l + 16)
                    wq = ring[:, 12, 0:3 * 576].rearrange("p (c n) -> p c n", c=3)
                    wkv = ring[:, 13, 0:2 * 768].rearrange("p (c n) -> p c n", c=2)
                    for j, (bank, tt, half) in enumerate(UQ_JOBS):
                        if j < 3:
                            pe.wait_ge(s["rope_mul"], 12 * l + 2 + j)
                        for c in range(3):
                            mm = pe.matmul(ps[:, bank, 0:288], lowT[:, c, tt * P:(tt + 1) * P],
                                           wq[:, c, half * 288:(half + 1) * 288], start=(c == 0), stop=(c == 2))
                        mm.then_inc(s["up_ps"], 1)
                    for j, (bank, tt, half) in enumerate(UKV_JOBS):
                        if j >= 2:
                            pe.wait_ge(s["rope_mul"], 12 * l + 3 + j)
                        for c in range(2):
                            mm = pe.matmul(ps[:, bank, 0:384], lowT[:, 3 + c, tt * P:(tt + 1) * P],
                                           wkv[:, c, half * 384:(half + 1) * 384], start=(c == 0), stop=(c == 1))
                        mm.then_inc(s["up_ps"], 1)
                    for j in (8, 9):
                        pe.wait_ge(s["rope_mul"], 12 * l + j - 1)
                        project_in(j)

                    def turn_qk(pos):
                        what, bank = T_JOBS[pos]
                        for c in range(2):
                            for tt in range(TT):
                                o = ps[:, bank, c * T + tt * P:c * T + (tt + 1) * P]
                                if what[0] in "qk":
                                    t = pe.transpose(o[0:MLA_QK], (qm if what[0] == "q" else km)[:, tt, 2 * int(what[1]) + c, :], ident)
                                else:
                                    c0 = {"sq": 0, "sqk": 2, "dq": 4, "dk": 6}[what] + c
                                    t = pe.transpose(o, rq[:, tt, c0 * P:(c0 + 1) * P], ident)
                                if pos == 0 and c == 0:
                                    t.then_inc(s["freed_a" if tt == 0 else "freed_b"], 1)
                        t.then_inc(s["T_ps"], 1)

                    pe.wait_ge(s["rope_add"], 12 * l + 4)
                    for pos in range(8):
                        if pos < 2:
                            pe.wait_ge(s["rope_mul"], 12 * l + 9 + pos)
                        if pos == 2:
                            pe.wait_ge(s["rope_add"], 12 * l + 10)
                            pe.wait_ge(s["q_nope"], 4 * l + 4)
                            pe.wait_ge(s["kv_sb"], 4 * l + 4)
                        if pos == 5:
                            pe.wait_ge(s["krope_sb"], l + 1)
                        if pos == 6:
                            pe.wait_ge(s["T_act"], 5 * l + 1)
                        if pos == 7:
                            pe.wait_ge(s["T_dve"], 5 * l + 1)
                        turn_qk(pos)
                    def project(j, k):
                        if k < NPLAIN // 2:
                            pe.wait_ge(*group_out(l, k))
                        mm = pe.matmul(ps[:, WOUT_BANKS[j], :], hT[:, k, j // 2 * P:(j // 2 + 1) * P],
                                       wslot(WOUT_SLOT[k // 2])[:, k % 2, j % 2 * 512:(j % 2 + 1) * 512],
                                       start=(k == 0), stop=(k == KD - 1))
                        if k == KD - 1:
                            mm.then_inc(s["wout_ps"], 1)

                    pe.wait_ge(s["T_act"], 5 * l + 4)
                    pe.wait_ge(s["T_dve"], 5 * l + 4)
                    for t_ in range(NMAPS + 5):
                        if t_ == 1:
                            turn_qk(8)
                        if t_ == 3:
                            pe.wait_ge(s["T_act"], 5 * l + 5)
                            pe.wait_ge(s["rope_add"], 12 * l + 12)
                            turn_qk(9)
                        if t_ == NPLAIN:
                            pe.wait_ge(s["T_dve"], 5 * l + 5)
                        if t_ < NMAPS:
                            q_of, k_all = MAPS[t_][0:2]
                            if t_ >= 3:
                                pe.wait_ge(s["prob_ready"], NMAPS * l + t_ - 2)
                            for qt in range(TT):
                                mm = pe.matmul(ps[:, t_ % 3, qt * T:(qt + 1) * T], q_of(qt), k_all, start=True, stop=True)
                            mm.then_inc(s["score_ps"], 1)
                        n_ = unit_at(t_ - 3)
                        if n_ is not None:
                            if n_ == 0:
                                pe.wait_ge(s["rope_mul"], 12 * l + 12)
                            pe.wait_ge(s["scaled"], NUNITS * l + n_ + 1)
                            if n_ >= 2:
                                pe.wait_ge(*turned(l, n_ - 2))
                            for kt in range(TT):
                                for qt in range(TT):
                                    t = pe.transpose(ps[:, 3 + n_ % 2, kt * T + qt * P:kt * T + (qt + 1) * P],
                                                     prob[unit_buf(n_)][:, qt, kt * P:(kt + 1) * P], ident)
                            t.then_inc(s["probT_ps"], 1)
                        if t_ == NPLAIN:
                            pe.wait_ge(s["landed_da"], 32 * n + 32)
                            pe.wait_ge(s["landed_wo"], 32 * l + 32)
                        if 0 <= t_ - NPLAIN < NPLAIN // 2:
                            project(0, t_ - NPLAIN)
                        g_ = group_at(t_ - 4)
                        if g_ is None:
                            continue
                        units = GROUPS[g_]
                        for n_ in units:
                            pe.wait_ge(*turned(l, n_))
                        if g_ >= 2:
                            pe.wait_ge(*group_out(l, g_ - 2))
                        bank = 5 + g_ % 2
                        if len(units) == 2:
                            for kt in range(TT):
                                for w, n_ in enumerate(units):
                                    mm = pe.matmul(ps[64 * w:64 * w + 64, bank, 0:T], MAPS[n_][2](kt),
                                                   probT[n_ % 4][:, kt, :], start=(kt == 0), stop=(kt == TT - 1))
                        else:
                            n_, = units
                            v_of = MAPS[NPLAIN + 2 * (n_ - NPLAIN)][2]
                            for qt in range(TT):
                                for kt in range(TT):
                                    mm = pe.matmul(ps[:, bank, qt * DV:(qt + 1) * DV], probT[n_ % 4][:, kt, qt * P:(qt + 1) * P],
                                                   v_of(kt), start=(kt == 0), stop=(kt == TT - 1))
                        mm.then_inc(s["o_ps"], 1)
                    pe.wait_ge(*turned(l, NUNITS - 1))
                    for k in range(NPLAIN // 2):
                        project(1, k)
                    pe.wait_ge(s["dnorm_ready"], l + 1)
                    for c in range(2):
                        for tt in range(TT):
                            t = pe.transpose(ps[:, 0, c * T + tt * P:c * T + (tt + 1) * P], odiff[:, tt, c * P:(c + 1) * P], ident)
                    t.then_inc(s["oT_ps"], 1)
                    pe.wait_ge(*group_out(l, len(GROUPS) - 1))
                    for k in range(NPLAIN // 2):
                        project(2, k)
                    pe.wait_ge(s["oT_dve"], l + 1)
                    for j in range(4):
                        for k in range(NPLAIN // 2 if j < 3 else 0, KD):
                            project(j, k)
                turn_h(l, 1)
                pe.wait_ge(s["hT_sb"], 8 * l + 8)
                for k in range(KD):
                    mm = pe.matmul(ps[0:G + NE, 4, 0:T], w_r[:, k, :], hT[:, k, :], start=(k == 0), stop=(k == KD - 1))
                mm.then_inc(s["logitT_ps"], 1)
                pe.wait_ge(s["logitT_sb"], l + 1)
                past(pe)
                for tt in range(TT):
                    t = pe.transpose(ps[:, 4, tt * 64:tt * 64 + G + NE], logitT[:, tt * P:(tt + 1) * P], ident[0:G + NE, 0:G + NE])
                t.then_inc(s["logit_ps"], 1)
                for tt in range(TT):
                    for half in range(2):
                        mm = pe.matmul(ps[:, 2 * tt + half, :], ident, x[:, tt, half * 512:(half + 1) * 512],
                                       start=True, stop=False, skip_group_check=True)
                pe.wait_ge(s["member_ready"], l + 1)
                pe.matmul(ps[:, 5, 0:16], tri, member[:, 0, :], start=True, stop=True)
                pe.matmul(ps[:, 5, 32:48], ones, member[:, 0, :], start=True, stop=False)
                pe.matmul(ps[:, 5, 32:48], tri, member[:, 1, :], start=False, stop=True)
                pe.matmul(ps[:, 5, 64:80], ones, member[:, 0, :], start=True, stop=False)
                pe.matmul(ps[:, 5, 64:80], ones, member[:, 1, :], start=False, stop=True).then_inc(s["rank_ps"], 1)
                npass = load_npass(pe, l)
                with pe.Fori(0, npass):
                    done = pe.snap(passes)
                    q_pair[0] = 0
                    prepare(done * (NIT + 1), False)
                    with pe.Fori(0, NIT) as i:
                        u = done * NIT + i
                        q = done * (NIT + 1) + i
                        use = l + 1 + u
                        pe.wait_ge(s["gath_sb"], 2 * q + 2)
                        for tt in range(TT):
                            t = pe.transpose(ps[:, 4, tt * P:(tt + 1) * P], pick[:, tt, :], ident)
                        t.then_inc(s["pickT_ps"], 1)
                        for which, (slot, land, bank) in enumerate(((0, "landed_a", 6), (4, "landed_b", 7))):
                            pe.wait_ge(s[land], 64 * use + 64)
                            if which == 0:
                                pe.wait_ge(s["comb_sb"], q + 1)
                            for k in range(KD):
                                for pr in range(2):
                                    mm = pe.matmul(ps[64 * pr:64 * pr + 64, bank, :].rearrange("p (w f) -> p w f", w=2),
                                                   hTg[:, k, 64 * pr:64 * pr + 64],
                                                   ring[:, slot + 2 * pr:slot + 2 * pr + 2, k * F:(k + 1) * F],
                                                   start=(k == 0), stop=(k == KD - 1))
                                    if which == 1 and k == 0 and pr == 0:
                                        mm.then_inc(s["freed_a"], 1)
                            mm.then_inc(s["guA_ps" if which == 0 else "guB_ps"], 1)
                        pe.wait_ge(s["pickT_sb"], u + 1)
                        pe.wait_ge(s["hid_a"], u + 1)
                        q_pair[0] = 4 * i + 4
                        prepare(q + 1)
                        pe.wait_ge(s["comb_sb"], q + 2)
                        for which in range(2):
                            if which == 1:
                                pe.wait_ge(s["hid_b"], u + 1)
                            for j in range(2):
                                t = pe.transpose(ps[:, 6 + which, j * P:(j + 1) * P], hid[which][:, j * P:(j + 1) * P], ident)
                            t.then_inc(s["hidT_ps"], 1)
                        pe.wait_ge(s["gath_sb"], 2 * q + 4)
                        for which, (slot, land) in enumerate(((8, "landed_da"), (10, "landed_db"))):
                            pe.wait_ge(s[land], 32 * (use if which == 0 else u) + 32)
                            pe.wait_ge(s["hidTa_sb" if which == 0 else "hidTb_sb"], u + 1)
                            for half in range(2):
                                for j in range(2):
                                    for pr in range(2):
                                        mm = pe.matmul(ps[64 * pr:64 * pr + 64, 4 + half, :],
                                                       hidT[which][:, j, 64 * pr:64 * pr + 64],
                                                       wslot(slot + pr)[:, j, half * 512:(half + 1) * 512],
                                                       start=(which == 0 and j == 0), stop=(which == 1 and j == 1),
                                                       skip_group_check=True)
                            mm.then_inc(s["freed_da" if which == 0 else "y_ps"], 1)
                        pe.wait_ge(s["y_act"], u + 1)
                        pe.wait_ge(s["y_dve"], u + 1)
                        for tt in range(TT):
                            for half in range(2):
                                mm = pe.matmul(ps[:, 2 * tt + half, :], pickT[:, tt * P:(tt + 1) * P], y_sb[:, half, :],
                                               start=False, stop=False, skip_group_check=True)
                                if tt == 0 and half == 0:
                                    mm.then_inc(s["freed_db"], 1)
                        mm.then_inc(s["acc_ready"], 1)
                    pe.reg_add(passes, passes, 1)

        @block.scalar
        def _(act):
            passes = act.alloc_register("act_passes")
            act.reg_mov(passes, 0)

            def norm_rows(l, which):
                act.activation(hAf[:, 0:D], x[:, 0, :], ACT.Square, accum_out=ssq[:, 0:1]).then_inc(s["sq_act"], 1)
                act.wait_ge(s["rms0_ready"], 2 * l + which + 1)
                act.activation(hA[:, 0, :, :], x[:, 0, :].rearrange("p (j k) -> p k j", k=KD), ACT.Copy,
                               scale=rs[:, 0:1]).then_inc(s["h_act"], 1)

            first = [
                (g_ffn[:, :, :], ffn_norm.rearrange("l (p k) -> p l k", k=KD)),
                (g_attn[:, :, :], attn_norm.rearrange("l (p k) -> p l k", k=KD)),
                (sink[:, :, :], swa_sink.rearrange("(a l) n -> a l n", a=1).broadcast_to([P, L, SWA_H])),
                (subln[0:64, :], diff_subln.rearrange("l p -> p l")),
                (subln[64:128, :], diff_subln.rearrange("l p -> p l")),
            ]
            first += [(lqk[:, n, :, :], v.rearrange("(a l) n -> a l n", a=1).broadcast_to([P, L, DQK]))
                      for n, v in enumerate((lq1, lk1, lq2, lk2))]
            for l in range(L):
                first += [(g_low[:, l, 0:3], mla_q_norm[l].rearrange("(c p) -> p c", p=P)),
                          (g_low[:, l, 3:5], mla_kv_norm[l].rearrange("(c p) -> p c", p=P))]
            assert len(first) == N_FIRST
            act.dma_start(cst[:, :], const).then_inc(s["const_landed"], 16)
            with nc.allow_non_contiguous_dma("small parameters"):
                for dst, src in first:
                    act.dma_start(dst, src).then_inc(s["params_landed"], 16)
            act.wait_ge(s["x_landed"], 16)
            act.wait_ge(s["cleared"], 2)
            with act.Fori(0, L) as l:
                n = l + act.snap(passes) * NIT
                norm_rows(l, 0)
                act.wait_ge(s["lam_sum"], l + 1)
                act.activation(lam[:, 2:4], lam[:, 0:2], ACT.Exp).then_inc(s["lam_exp"], 1)
                act.wait_ge(s["freed_up"], 2 * l + 1)
                act.wait_ge(s["landed_b"], 64 * n + 64)
                past(act)
                load_up(act, l)
                for j in range(4):
                    w, c0 = (MLA_QR, 0) if j < 2 else (MLA_KVR, MLA_QR)
                    act.wait_ge(s["u_ps"], 10 * l + j + 1)
                    act.activation(msf[:, 0:w], ps[:, j, 0:w], ACT.Square, accum_out=ssc[:, j:j + 1]).then_inc(s["low_sq"], 1)
                    act.drain()
                for j in range(4):
                    w, c0 = (MLA_QR, 0) if j < 2 else (MLA_KVR, MLA_QR)
                    act.wait_ge(s["low_rms"], 2 * l + 1 + j // 2)
                    act.activation(low[:, j % 2, c0:c0 + w], ps[:, j, 0:w], ACT.Copy,
                                   scale=rsc[:, j:j + 1]).then_inc(s["low_ready"], 1)
                def values_out(j):
                    act.wait_ge(s["u_ps"], 10 * l + j + 1)
                    bank, tt = IN_JOBS[j][0:2]
                    if j < 8:
                        act.copy(vsd[:, tt, 0:128], ps[:, bank, 0:128]).then_inc(s["v_sb"], 1)
                    else:
                        act.copy(vsd[:, tt, 128:384], ps[:, bank, 256:512]).then_inc(s["v_sb"], 1)

                row = lambda v: v[bass.ds(l, 1)]
                second = [(rbias[:, 0:G], row(router_group_bias).broadcast_to([P, G])),
                          (rbias[:, G:G + NE], row(router_expert_bias).broadcast_to([P, NE])),
                          (w_r[:, :, 0:G], row(router_group.rearrange("l (p k) g -> l p k g", k=KD)).rearrange("a p k g -> (a p) k g")),
                          (w_r[:, :, G:G + NE], row(router_expert.rearrange("l (p k) g -> l p k g", k=KD)).rearrange("a p k g -> (a p) k g")),
                          (g_fin[:, :], final_norm.rearrange("(a n) -> a n", a=1).broadcast_to([P, D]))]
                assert len(second) == N_SECOND
                with nc.allow_non_contiguous_dma("small parameters"):
                    for dst, src in second:
                        act.dma_start(dst, src).then_inc(s["router_landed"], 16)
                values_out(6)
                values_out(7)
                for j, (bank, tt, half) in enumerate(UQ_JOBS):
                    act.wait_ge(s["up_ps"], 8 * l + j + 1)
                    v = ps[:, bank, 0:288].rearrange("p (h d) -> p h d", h=3)
                    act.copy(qm[:, tt, 3 * half:3 * half + 3, 0:NOPE], v[:, :, 0:NOPE]).then_inc(s["q_nope"], 1)
                for j, (bank, tt, half) in enumerate(UKV_JOBS):
                    act.wait_ge(s["up_ps"], 8 * l + j + 5)
                    v = ps[:, bank, 0:384].rearrange("p (h d) -> p h d", h=3)
                    act.copy(km[:, tt, 3 * half:3 * half + 3, 0:NOPE], v[:, :, 0:NOPE])
                    act.copy(vm[:, tt, 192 * half:192 * half + 192].rearrange("p (h d) -> p h d", h=3),
                             v[:, :, NOPE:128]).then_inc(s["kv_sb"], 1)
                values_out(8)
                values_out(9)
                for pos in (0, 2, 4, 6):
                    act.wait_ge(s["T_ps"], 10 * l + pos + 1)
                    take_turned(act, pos).then_inc(s["T_act"], 1)
                for t_ in range(NMAPS + 3):
                    if t_ < NMAPS:
                        kind, n = MAPS[t_][4:6]
                        act.wait_ge(s["nmax_ready"], NMAPS * l + t_ + 1)
                        if t_ >= 4:
                            act.wait_ge(s["probT_ps"], NUNITS * l + unit_of(t_ - 4) + 1)
                        if kind == "swa":
                            act.activation(esink[:, n, :], nmax[:, t_, :], ACT.Exp,
                                           bias=sink[:, bass.ds(l, 1), n:n + 1].rearrange("p a n -> p (a n)"))
                        for qt in range(TT):
                            src = masked[n % 2][:, qt, :] if kind == "swa" else ps[:, t_ % 3, qt * T:(qt + 1) * T]
                            i = act.activation(prob[t_ % 4][:, qt, :], src, ACT.Exp, bias=nmax[:, t_, qt:qt + 1],
                                               accum_out=psum_[:, t_, qt:qt + 1])
                        i.then_inc(s["prob_ready"], 1)
                    if t_ == 1:
                        act.wait_ge(s["T_ps"], 10 * l + 9)
                        take_turned(act, 8).then_inc(s["T_act"], 1)
                    m = unit_at(t_ - 3)
                    if m is not None and not by_dve(m):
                        act.wait_ge(s["probT_ps"], NUNITS * l + m + 1)
                        if m >= 4:
                            act.wait_ge(s["o_ps"], len(GROUPS) * l + group_of(m - 4) + 1)
                        act.copy(probT[m % 4], ps[:, 3 + m % 2, :].rearrange("p (k t) -> p k t", k=TT)).then_inc(s["probT_act"], 1)
                    g_ = group_at(t_ - 4)
                    if g_ is not None and len(GROUPS[g_]) == 2:
                        act.wait_ge(s["o_ps"], len(GROUPS) * l + g_ + 1)
                        act.copy(hT[:, g_, :], ps[:, 5 + g_ % 2, 0:T]).then_inc(s["o_act"], 1)
                act.wait_ge(s["x_mixed"], 4 * l + 2)
                norm_rows(l, 1)
                act.wait_ge(s["rt_dve"], 2 * l + 1)
                for tt in range(TT):
                    i = act.activation(gexp[:, tt, :], gl8[:, tt, 0:G], ACT.Exp, bias=ngm[:, tt:tt + 1],
                                       accum_out=gsum[:, tt:tt + 1])
                i.then_inc(s["rt_exp"], 1)
                act.wait_ge(s["rt_dve"], 2 * l + 2)
                act.activation(wts[:, 1, :], wts[:, 0, :], ACT.Exp).then_inc(s["rt_exp"], 1)
                npass = load_npass(act, l)
                with act.Fori(0, npass):
                    done = act.snap(passes)
                    with act.Fori(0, NIT) as i:
                        u = done * NIT + i
                        act.wait_ge(s["pickT_ps"], u + 1)
                        act.copy(pickT, ps[:, 4, 0:T]).then_inc(s["pickT_sb"], 1)
                        act.wait_ge(s["guA_ps"], u + 1)
                        act.activation(sil[0], ps[:, 6, 0:F], ACT.Silu).then_inc(s["silu_a"], 1)
                        act.wait_ge(s["guB_ps"], u + 1)
                        act.activation(sil[1], ps[:, 7, 0:F], ACT.Silu).then_inc(s["silu_b"], 1)
                        act.wait_ge(s["hidT_ps"], 2 * u + 1)
                        act.copy(hidT[0], ps[:, 6, 0:T].rearrange("p (j s) -> p j s", j=2)).then_inc(s["hidTa_sb"], 1)
                        act.wait_ge(s["y_ps"], u + 1)
                        act.copy(y_sb[:, 1, :], ps[:, 5, :]).then_inc(s["y_act"], 1)
                    act.reg_add(passes, passes, 1)
                act.wait_ge(s["acc_ready"], act.snap(passes) * NIT)
                act.copy(x[:, 0, :].rearrange("p (b n) -> p b n", b=2), ps[:, 0:2, :]).then_inc(s["x_act"], 1)
                act.drain()
            act.activation(hAf[:, 0:D], x[:, 0, :], ACT.Square, accum_out=ssq[:, 0:1]).then_inc(s["sq_act"], 1)

        @block.gpsimd
        def _(pool):
            pool.memset(nhalf[:, :], -0.5).then_inc(s["cleared"], 1)
            pool.drain()

            def rms(out_, in_, width, n, sem):
                past(pool)
                pool.tensor_scalar(out_, in_, 1.0 / width, EPS, ALU.mult, ALU.add)
                pool.drain()
                pool.tensor_tensor(out_, out_, nhalf[:, 0:n], ALU.pow).then_inc(sem, 1)
                pool.drain()

            def rms_rows(count):
                pool.wait_ge(s["sq_act"], count)
                rms(rs[:, 0:1], ssq[:, 0:1], D, 1, s["rms0_ready"])
                pool.wait_ge(s["sq_dve"], count)
                rms(rs[:, 1:2], ssq[:, 1:2], D, 1, s["rms1_ready"])

            def add(out_, r, w, shape=None):
                a, b = (v[:, 0:w] for v in rope_tmps(r))
                return pool.tensor_tensor(out_, shape(a) if shape else a, shape(b) if shape else b, ALU.add)

            with pool.Fori(0, L) as l:
                rms_rows(2 * l + 1)
                for half, w in ((0, MLA_QR), (1, MLA_KVR)):
                    pool.wait_ge(s["low_sq"], 4 * l + 2 * half + 2)
                    rms(rsc[:, 2 * half:2 * half + 2], ssc[:, 2 * half:2 * half + 2], w, 2, s["low_rms"])
                heads = lambda n: (lambda v: v.rearrange("p (h d) -> p h d", h=n))
                for r in range(12):
                    pool.wait_ge(s["rope_mul"], 12 * l + r + 1)
                    tt = r % 2
                    if r < 2:
                        i = add(kro[:, tt, :], r, ROPE)
                    elif r < 4:
                        a, b = tmpA[tt][:, 0:384], tmpB[tt][:, 0:384]
                        f = lambda v: v.rearrange("p (b c d) -> p b c d", b=2, c=3)
                        pool.tensor_tensor(rq[:, tt, 0:384].rearrange("p (c b d) -> p b c d", b=2, c=3), f(a), f(b), ALU.add)
                        i = pool.tensor_tensor(rq[:, tt, 384:512], tmpA[tt][:, 384:512], tmpB[tt][:, 384:512], ALU.add)
                    elif r < 6 or r >= 10:
                        c0 = 512 if r < 6 else 768
                        i = add(rq[:, tt, c0:c0 + 256], r, 256)
                    else:
                        _, t2, half = UQ_JOBS[r - 6]
                        i = add(qm[:, t2, 3 * half:3 * half + 3, NOPE:MLA_QK], r, 3 * ROPE, heads(3))
                    i.then_inc(s["rope_add"], 1)
                    if r == 1:
                        pool.drain()
                    if r == 3:
                        for t2 in range(TT):
                            i = pool.tensor_copy(km[:, t2, :, NOPE:MLA_QK],
                                                 kro[:, t2, :].unsqueeze(1).broadcast_to([P, MLA_H, ROPE]))
                        i.then_inc(s["krope_sb"], 1)
                pool.wait_ge(s["dsq_ready"], l + 1)
                rms(drs[:, :], dssq[:, :], DV, 8, s["drms_ready"])
                rms_rows(2 * l + 2)
            rms_rows(2 * L + 1)

        @block.vector
        def _(dve):
            passes = dve.alloc_register("dve_passes")
            dve.reg_mov(passes, 0)

            def norm_rows(l, which):
                dve.tensor_tensor_reduce(hAf[:, D:2 * D], x[:, 1, :], x[:, 1, :], 1.0, 0.0, ALU.mult, ALU.add,
                                         ssq[:, 1:2]).then_inc(s["sq_dve"], 1)
                dve.wait_ge(s["rms1_ready"], 2 * l + which + 1)
                dve.tensor_scalar(hA[:, 1, :, :], x[:, 1, :].rearrange("p (j k) -> p k j", k=KD), rs[:, 1:2], None,
                                  ALU.mult).then_inc(s["h_dve"], 1)

            def turn_out(l, which, gain):
                g = lay(gain, l)
                for b in range(4):
                    dve.wait_ge(s["hT_ps"], 8 * l + 4 * which + b + 1)
                    dve.tensor_tensor(hT[:, 2 * b:2 * b + 2, :], ps[:, b, :].rearrange("p (c t) -> p c t", c=2),
                                      g[:, 2 * b:2 * b + 2].unsqueeze(2).broadcast_to([P, 2, T]), ALU.mult).then_inc(s["hT_sb"], 1)

            def rope(l, r, tt, src, nh, dim):
                h = dim // 2
                if r >= 2:
                    dve.wait_ge(s["rope_add"], 12 * l + r - 1)
                a, b = (v[:, 0:nh * dim] for v in rope_tmps(r))
                cos, sin, nsin = (table(dim, n, tt) for n in range(3))
                dve.tensor_tensor(a.rearrange("p (h d) -> p h d", d=h) if len(src.shape) == 2 else
                                  a.rearrange("p (h w d) -> p h w d", w=2, d=h),
                                  src.rearrange("p (h d) -> p h d", d=h) if len(src.shape) == 2 else
                                  src.rearrange("p h (w d) -> p h w d", w=2),
                                  cos.unsqueeze(1).broadcast_to([P, 2 * nh, h]) if len(src.shape) == 2 else
                                  cos.unsqueeze(1).unsqueeze(1).broadcast_to([P, nh, 2, h]), ALU.mult)
                bv = b.rearrange("p (h w d) -> p h w d", w=2, d=h)
                sv = src.rearrange("p (h w d) -> p h w d", w=2, d=h) if len(src.shape) == 2 else \
                    src.rearrange("p h (w d) -> p h w d", w=2)
                dve.tensor_tensor(bv[:, :, 0, :], sv[:, :, 1, :], nsin.unsqueeze(1).broadcast_to([P, nh, h]), ALU.mult)
                dve.tensor_tensor(bv[:, :, 1, :], sv[:, :, 0, :], sin.unsqueeze(1).broadcast_to([P, nh, h]),
                                  ALU.mult).then_inc(s["rope_mul"], 1)

            dve.memset(kps[:, :, :], 0.0)
            dve.memset(kpd[:, :, :], 0.0)
            dve.memset(gl8[:, :, :], NEG)
            dve.memset(key[:, :, :], -1.0)
            dve.memset(comb[:, :, :], 0.0).then_inc(s["cleared"], 1)
            dve.wait_ge(s["params_landed"], 16 * N_FIRST)
            dve.wait_ge(s["const_landed"], 16)
            dve.tensor_scalar(nsink[:, :, :], sink[:, :, :], -1.0, None, ALU.mult)
            dve.tensor_tensor(sublg[:, :], subln[:, :], cst[:, O_LAM + L:O_LAM + 2 * L], ALU.mult)
            dve.drain()
            dve.wait_ge(s["x_landed"], 16)
            with dve.Fori(0, L) as l:
                norm_rows(l, 0)
                for n in range(2):
                    q, k = (lqk[:, 2 * n + c, bass.ds(l, 1), :].rearrange("p a n -> p (a n)") for c in range(2))
                    dve.tensor_tensor(msf[:, n * DQK:(n + 1) * DQK], q, k, ALU.mult)
                dve.drain()
                i = dve.tensor_reduce(lam[:, 0:2], msf[:, 0:2 * DQK].rearrange("p (n d) -> p n d", n=2), AX, ALU.add)
                i.then_inc(s["lam_sum"], 1)
                dve.wait_ge(s["lam_exp"], l + 1)
                dve.tensor_tensor(neglam[:, :], lam[:, 3:4], lam[:, 2:3], ALU.subtract)
                dve.drain()
                dve.tensor_tensor(neglam[:, :], neglam[:, :], cst[:, bass.ds(l + O_LAM, 1)], ALU.subtract)
                turn_out(l, 0, g_attn)
                for tt in range(TT):
                    dve.wait_ge(s["low_ready"], 4 * l + 3 + tt)
                    rope(l, tt, tt, ps[:, 2 + tt, MLA_KVR:MLA_KVR + ROPE], 1, 32)
                for tt in range(TT):
                    dve.wait_ge(s["u_ps"], 10 * l + 5 + tt)
                    rope(l, 2 + tt, tt, ps[:, 4 + tt, :], 8, 64)
                for b in range(3):
                    nch = 2 if b < 2 else 1
                    dve.wait_ge(s["lowT_ps"], 3 * l + b + 1)
                    g = lay(g_low, l)
                    dve.tensor_tensor(lowT[:, 2 * b:2 * b + nch, :], ps[:, LOWT_BANKS[b], 0:nch * T].rearrange("p (c t) -> p c t", c=nch),
                                      g[:, 2 * b:2 * b + nch].unsqueeze(2).broadcast_to([P, nch, T]), ALU.mult).then_inc(s["lowT_sb"], 1)
                for tt in range(TT):
                    dve.wait_ge(s["v_sb"], 4 * l + 1 + tt)
                    rope(l, 4 + tt, tt, ps[:, IN_JOBS[6 + tt][0], 128:384], 8, 32)
                for j, (bank, tt, half) in enumerate(UQ_JOBS):
                    dve.wait_ge(s["q_nope"], 4 * l + j + 1)
                    rope(l, 6 + j, tt, ps[:, bank, 0:288].rearrange("p (h d) -> p h d", h=3)[:, :, NOPE:MLA_QK], 3, 32)
                for tt in range(TT):
                    dve.wait_ge(s["v_sb"], 4 * l + 3 + tt)
                    rope(l, 10 + tt, tt, ps[:, IN_JOBS[8 + tt][0], 0:256], 8, 32)
                for pos in (1, 3, 5, 7):
                    dve.wait_ge(s["T_ps"], 10 * l + pos + 1)
                    take_turned(dve, pos).then_inc(s["T_dve"], 1)
                def add_sink(m):
                    dve.wait_ge(s["prob_ready"], NMAPS * l + m + 1)
                    dve.tensor_tensor(psum_[:, m, :], psum_[:, m, :], esink[:, MAPS[m][5], :], ALU.add)

                for t_ in range(NMAPS + 5):
                    if t_ < NMAPS:
                        kind, n = MAPS[t_][4:6]
                        v = ps[:, t_ % 3, :].rearrange("p (t k) -> p t k", t=TT)
                        dve.wait_ge(s["score_ps"], NMAPS * l + t_ + 1)
                        if kind == "swa":
                            dve.wait_ge(s["prob_ready"], NMAPS * l + t_ - 1)
                            past(dve)
                            for qt in range(TT):
                                dve.tensor_tensor_reduce(masked[n % 2][:, qt, :], v[:, qt, :], mask[:, qt, :], 1.0, NEG, ALU.add, ALU.max,
                                                         rmax[:, t_, qt:qt + 1])
                            if t_ - 1 >= 0 and MAPS[t_ - 1][4] == "swa":
                                add_sink(t_ - 1)
                            dve.drain()
                            ns = nsink[:, bass.ds(l, 1), n:n + 1].rearrange("p a n -> p (a n)")
                            i = dve.tensor_scalar(nmax[:, t_, :], rmax[:, t_, :], -1.0, ns, ALU.mult, ALU.min)
                        else:
                            i = dve.tensor_reduce(nmax[:, t_, :], v, AX, ALU.max, negate=True)
                        i.then_inc(s["nmax_ready"], 1)
                    if t_ == 3:
                        dve.wait_ge(s["T_ps"], 10 * l + 10)
                        take_turned(dve, 9).then_inc(s["T_dve"], 1)
                    m = unit_at(t_ - 3)
                    if m is not None and by_dve(m):
                        dve.wait_ge(s["probT_ps"], NUNITS * l + m + 1)
                        if m >= 4:
                            dve.wait_ge(s["o_ps"], len(GROUPS) * l + group_of(m - 4) + 1)
                        dve.tensor_copy(probT[m % 4], ps[:, 3 + m % 2, :].rearrange("p (k t) -> p k t", k=TT)).then_inc(s["probT_dve"], 1)
                    m = t_ - 1
                    if 0 <= m < NMAPS:
                        kind, n = MAPS[m][4:6]
                        dve.wait_ge(s["prob_ready"], NMAPS * l + m + 1)
                        if kind == "swa" and MAPS[t_][4] != "swa":
                            add_sink(m)
                            dve.drain()
                        i = dve.reciprocal(rinv[:, m, :], psum_[:, m, :])
                        dve.drain()
                        if m < NPLAIN:
                            for qt in range(TT):
                                i = dve.tensor_scalar(prob[m % 4][:, qt, :], prob[m % 4][:, qt, :], rinv[:, m, qt:qt + 1],
                                                      None, ALU.mult)
                            i.then_inc(s["scaled"], 1)
                        elif n % 2 == 1:
                            dve.tensor_scalar(rinv[:, m, :], rinv[:, m, :], neglam[:, 0:1], None, ALU.mult)
                            p0, p1 = prob[(m - 1) % 4], prob[m % 4]
                            for qt in range(TT):
                                dve.tensor_scalar(p0[:, qt, :], p0[:, qt, :], rinv[:, m - 1, qt:qt + 1], None, ALU.mult)
                            dve.drain()
                            for qt in range(TT):
                                i = dve.scalar_tensor_tensor(out=p0[:, qt, :], in0=p1[:, qt, :], scalar=rinv[:, m, qt:qt + 1],
                                                             in1=p0[:, qt, :], op0=ALU.mult, op1=ALU.add)
                            i.then_inc(s["scaled"], 1)
                    g_ = group_at(t_ - 4)
                    if g_ is not None and len(GROUPS[g_]) == 1:
                        units = GROUPS[g_]
                        dve.wait_ge(s["o_ps"], len(GROUPS) * l + g_ + 1)
                        if len(units) == 1:
                            h = units[0] - NPLAIN
                            i = dve.tensor_copy(odiff[:, :, h * DV:(h + 1) * DV],
                                                ps[:, 5 + g_ % 2, 0:TT * DV].rearrange("p (t d) -> p t d", t=TT))
                        i.then_inc(s["o_dve"], 1)
                dve.drain()
                od = odiff
                dve.tensor_tensor(ms[:, :, :], od, od, ALU.mult)
                dve.drain()
                dve.tensor_reduce(dssq[:, :], msf.rearrange("p (h d) -> p h d", d=DV), AX, ALU.add).then_inc(s["dsq_ready"], 1)
                dve.wait_ge(s["drms_ready"], l + 1)
                for tt in range(TT):
                    v = od[:, tt, :].rearrange("p (h d) -> p h d", d=DV)
                    i = dve.tensor_tensor(v, v, drs[:, 4 * tt:4 * tt + 4].unsqueeze(2).broadcast_to([P, 4, DV]), ALU.mult)
                i.then_inc(s["dnorm_ready"], 1)
                dve.wait_ge(s["oT_ps"], l + 1)
                dve.tensor_scalar(hT[:, 6:8, :], ps[:, 0, :].rearrange("p (c t) -> p c t", c=2), col(sublg, l), None,
                                  ALU.mult).then_inc(s["oT_dve"], 1)
                for j in range(4):
                    tt, half = j // 2, j % 2
                    dve.wait_ge(s["wout_ps"], 4 * l + j + 1)
                    v = x[:, tt, half * 512:(half + 1) * 512]
                    dve.tensor_tensor(v, v, ps[:, WOUT_BANKS[j], :], ALU.add).then_inc(s["x_mixed"], 1)
                dve.drain()
                norm_rows(l, 1)
                dve.wait_ge(s["router_landed"], 16 * N_SECOND * l + 16 * N_SECOND)
                turn_out(l, 1, g_ffn)
                dve.wait_ge(s["logitT_ps"], l + 1)
                dve.tensor_copy(logitT, ps[0:G + NE, 4, 0:T]).then_inc(s["logitT_sb"], 1)
                dve.wait_ge(s["logit_ps"], l + 1)
                lg = ps[:, 4, 0:128].rearrange("p (t n) -> p t n", t=TT)
                bias = rbias[:, :].unsqueeze(1)
                dve.tensor_tensor(gl8[:, :, 0:G], lg[:, :, 0:G], bias[:, :, 0:G].broadcast_to([P, TT, G]), ALU.add)
                dve.tensor_tensor(el[:, :, :], lg[:, :, G:G + NE], bias[:, :, G:G + NE].broadcast_to([P, TT, NE]), ALU.add)
                dve.drain()
                for tt in range(TT):
                    dve.max(gtop[:, tt, :], gl8[:, tt, :])
                dve.drain()
                dve.tensor_scalar(ngm[:, :].unsqueeze(2), gtop[:, :, 0:1], -1.0, None, ALU.mult).then_inc(s["rt_dve"], 1)
                for tt in range(TT):
                    dve.max_index(gidx[:, tt, :], gtop[:, tt, :], gl8[:, tt, :])
                dve.drain()
                dve.tensor_copy(fidx[:, 0, :, :], gidx[:, :, :])
                dve.drain()
                dve.tensor_tensor(ohg[:, :, :], iota[:, 0:G].unsqueeze(1).broadcast_to([P, TT, G]),
                                  fidx[:, 0, :, 0:1].broadcast_to([P, TT, G]), ALU.is_equal)
                dve.drain()
                dve.tensor_tensor(prod[:, :, :, :], el[:, :, :].rearrange("p t (g e) -> p t g e", g=G),
                                  ohg[:, :, :].unsqueeze(3).broadcast_to([P, TT, G, E]), ALU.mult)
                dve.drain()
                dve.tensor_reduce(esel[:, :, :], prod[:, :, :, :].rearrange("p t g e -> p t e g"), AX, ALU.add)
                dve.drain()
                for tt in range(TT):
                    dve.max(etop[:, tt, :], esel[:, tt, :])
                dve.drain()
                dve.tensor_tensor(wts[:, 0, :].unsqueeze(2), etop[:, :, 1:2], etop[:, :, 0:1], ALU.subtract).then_inc(s["rt_dve"], 1)
                for tt in range(TT):
                    dve.max_index(eidx[:, tt, :], etop[:, tt, :], esel[:, tt, :])
                dve.drain()
                dve.tensor_copy(fidx[:, 1, :, :], eidx[:, :, :])
                dve.drain()
                io8 = iota[:, 0:E].unsqueeze(1).broadcast_to([P, TT, E])
                for c in range(2):
                    dve.tensor_tensor(oh[:, c, :, :], io8, fidx[:, 1, :, c:c + 1].broadcast_to([P, TT, E]), ALU.is_equal)
                dve.drain()
                dve.tensor_tensor(oh[:, 2, :, :], oh[:, 0, :, :], oh[:, 1, :, :], ALU.add)
                dve.drain()
                dve.tensor_reduce(pmax[:, :, :], oh[:, 2, :, :].rearrange("p t (q w) -> p t q w", w=2), AX, ALU.max)
                dve.drain()
                dve.tensor_tensor(member[:, :, :].rearrange("p t (g q) -> p t g q", g=G),
                                  pmax[:, :, :].unsqueeze(2).broadcast_to([P, TT, G, 4]),
                                  ohg[:, :, :].unsqueeze(3).broadcast_to([P, TT, G, 4]), ALU.mult).then_inc(s["member_ready"], 1)
                dve.wait_ge(s["rt_exp"], 2 * l + 2)
                dve.tensor_scalar(wts[:, 2, :], wts[:, 1, :], 1.0, None, ALU.add)
                dve.drain()
                dve.tensor_tensor(wts[:, 2, :], wts[:, 2, :], gsum[:, :], ALU.mult)
                dve.drain()
                dve.reciprocal(wts[:, 3, :], wts[:, 2, :])
                dve.drain()
                dve.tensor_tensor(wts[:, 4, :], wts[:, 3, :], wts[:, 1, :], ALU.mult)
                dve.drain()
                for c in range(2):
                    dve.tensor_tensor(oh[:, 3 + c, :, :], oh[:, c, :, :], wts[:, 3 + c, :].unsqueeze(2).broadcast_to([P, TT, E]), ALU.mult)
                dve.drain()
                dve.tensor_tensor(oh[:, 3, :, :], oh[:, 3, :, :], oh[:, 4, :, :], ALU.add)
                dve.drain()
                for tt in range(TT):
                    dve.tensor_tensor(comb[:, tt, 0:NE].rearrange("p (g e) -> p g e", g=G),
                                      oh[:, 3, tt, :].unsqueeze(1).broadcast_to([P, G, E]),
                                      ohg[:, tt, :].unsqueeze(2).broadcast_to([P, G, E]), ALU.mult)
                dve.wait_ge(s["rank_ps"], l + 1)
                for tt in range(TT):
                    dve.scalar_tensor_tensor(out=key[:, tt, 0:NPAIR], in0=ps[:, 5, 32 * tt:32 * tt + NPAIR], scalar=1.0,
                                             in1=member[:, tt, :], op0=ALU.add, op1=ALU.mult)
                dve.tensor_reduce(cnt[:, 0:1], ps[:, 5, 64:64 + NPAIR], AX, ALU.max)
                dve.drain()
                dve.tensor_scalar(key[:, :, 0:NPAIR], key[:, :, 0:NPAIR], 1.0, None, ALU.subtract)
                dve.tensor_scalar(cnt[:, 1:2], cnt[:, 0:1], float(SLOTS), None, ALU.is_gt)
                dve.tensor_scalar(cnt[:, 2:3], cnt[:, 0:1], float(2 * SLOTS), None, ALU.is_gt)
                dve.tensor_scalar(cnt[:, 3:4], cnt[:, 0:1], float(3 * SLOTS), None, ALU.is_gt)
                dve.drain()
                dve.tensor_reduce(cnt[:, 0:1], cnt[:, 1:4], AX, ALU.add)
                dve.drain()
                dve.tensor_scalar(npass_t[:, :], cnt[:, 0:1], 1.0, None, ALU.add).then_inc(s["routed"], 1)
                npass = load_npass(dve, l)

                def build_pick(pair):
                    kv = key[:, :, bass.ds(pair, 2)].unsqueeze(3).broadcast_to([P, TT, 2, SLOTS])
                    for tt in range(TT):
                        i = dve.tensor_tensor(pick[:, tt, :].rearrange("p (q s) -> p q s", q=2),
                                              iota.unsqueeze(1).broadcast_to([P, 2, SLOTS]), kv[:, tt], ALU.is_equal)
                    i.then_inc(s["pick_ready"], 1)

                def gather_out(l, q):
                    dve.wait_ge(s["comb_ps"], q + 1)
                    dve.tensor_copy(cc[0:64, :], ps[0:64, 6, 0:2])
                    dve.tensor_copy(cc[64:128, :], ps[64:128, 6, 2:4]).then_inc(s["comb_sb"], 1)
                    g = lay(g_ffn, l)
                    for c, (bank, k0) in enumerate(((5, 0), (4, 4))):
                        dve.wait_ge(s["gath_ps"], 2 * q + c + 1)
                        dve.tensor_tensor(hTg[:, k0:k0 + 4, :], ps[:, bank, :].rearrange("p (k s) -> p k s", k=4),
                                          g[:, k0:k0 + 4].unsqueeze(2).broadcast_to([P, 4, P]), ALU.mult).then_inc(s["gath_sb"], 1)

                with dve.Fori(0, npass):
                    done = dve.snap(passes)
                    dve.drain()
                    build_pick(0)
                    gather_out(l, done * (NIT + 1))
                    with dve.Fori(0, NIT) as i:
                        u = done * NIT + i
                        q = done * (NIT + 1) + i
                        dve.wait_ge(s["pickT_ps"], u + 1)
                        build_pick(2 * i + 2)
                        dve.drain()
                        dve.wait_ge(s["silu_a"], u + 1)
                        dve.scalar_tensor_tensor(out=hid[0], in0=sil[0], scalar=cc[:, 0:1], in1=ps[:, 6, F:2 * F],
                                                 op0=ALU.mult, op1=ALU.mult).then_inc(s["hid_a"], 1)
                        dve.wait_ge(s["silu_b"], u + 1)
                        dve.scalar_tensor_tensor(out=hid[1], in0=sil[1], scalar=cc[:, 1:2], in1=ps[:, 7, F:2 * F],
                                                 op0=ALU.mult, op1=ALU.mult).then_inc(s["hid_b"], 1)
                        dve.drain()
                        gather_out(l, q + 1)
                        dve.wait_ge(s["hidT_ps"], 2 * u + 2)
                        dve.tensor_copy(hidT[1], ps[:, 7, 0:T].rearrange("p (j s) -> p j s", j=2)).then_inc(s["hidTb_sb"], 1)
                        dve.wait_ge(s["y_ps"], u + 1)
                        dve.tensor_copy(y_sb[:, 0, :], ps[:, 4, :]).then_inc(s["y_dve"], 1)
                    dve.drain()
                    dve.tensor_scalar(key[:, :, 0:NPAIR], key[:, :, 0:NPAIR], float(SLOTS), None, ALU.subtract)
                    dve.reg_add(passes, passes, 1)
                dve.wait_ge(s["acc_ready"], dve.snap(passes) * NIT)
                dve.tensor_copy(x[:, 1, :].rearrange("p (b n) -> p b n", b=2), ps[:, 2:4, :]).then_inc(s["x_dve"], 1)
                dve.drain()
            dve.tensor_tensor_reduce(hAf[:, D:2 * D], x[:, 1, :], x[:, 1, :], 1.0, 0.0, ALU.mult, ALU.add,
                                     ssq[:, 1:2]).then_inc(s["sq_dve"], 1)
            dve.wait_ge(s["rms0_ready"], 2 * L + 1)
            dve.wait_ge(s["rms1_ready"], 2 * L + 1)
            dve.wait_ge(s["x_act"], L)
            for tt in range(TT):
                dve.scalar_tensor_tensor(out=hT[:, 4 * tt:4 * tt + 4, :].rearrange("p k n -> p (k n)"), in0=x[:, tt, :],
                                         scalar=rs[:, tt:tt + 1], in1=g_fin[:, :], op0=ALU.mult,
                                         op1=ALU.mult).then_inc(s["out_ready"], 1)


N_FIRST, N_SECOND = 9 + 2 * L, 5

_INS = ['x', 'attn_norm', 'w_in', 'mla_q_norm', 'mla_kv_norm', 'mla_w_uq', 'mla_w_ukv', 'swa_sink', 'diff_lq1', 'diff_lk1',
        'diff_lq2', 'diff_lk2', 'diff_subln', 'w_out', 'ffn_norm', 'router_group', 'router_group_bias', 'router_expert',
        'router_expert_bias', 'w_gate', 'w_up', 'w_down', 'final_norm']


def kernel(**inputs):
    import concourse.bacc as _bacc
    from concourse.bass_utils import run_bass_kernel_spmd as _run

    nc = _bacc.Bacc("TRN2", target_bir_lowering=False, num_devices=1)
    arrays = {"const_dram": constants()}
    for name in _INS:
        arrays[f"in_{name}_dram"] = np.ascontiguousarray(inputs[name])
    args = [nc.dram_tensor(n, a.shape, mybir.dt.from_np(a.dtype), kind="ExternalInput").ap() for n, a in arrays.items()]
    args.append(nc.dram_tensor("out_0_dram", (1, T, D), F32, kind="ExternalOutput").ap())
    encoder_kernel(nc, *args)
    r = _run(nc, [arrays], core_ids=[0])
    return r.results[0]["out_0_dram"]
```
